# Optimizing a Trainium2 kernel written in Bass

```python
import math
import jax, jax.numpy as jnp
from jax import lax
import numpy as np

D_MODEL = 2048
BATCH = 1
SEQ = 256
DEPTH = 2

ATT_HEADS = 8
ATT_QK_DIM = 64
ATT_V_DIM = 2 * ATT_QK_DIM
ATT_WIDTH = ATT_HEADS * ATT_V_DIM
Q_BLOCK = 128
ROPE_THETA = 500000.0
ROT_DIM = ATT_QK_DIM // 4
POOL_WINDOWS = (2, 4, 8, 16)
N_POOL = len(POOL_WINDOWS)
POOL_CH = 128
POOL_WIDTH = N_POOL * POOL_CH
SSM_GROUP_CH = 16
SSM_WIDTH = 512
SSM_GROUPS = SSM_WIDTH // SSM_GROUP_CH
SSM_STATE = 64
D_FF = 4 * D_MODEL
N_BRANCH = 3
DEEPNORM_ALPHA = (2.0 * DEPTH) ** 0.25
DEEPNORM_BETA = (8.0 * DEPTH) ** -0.25
LN_EPS = 1e-5

Q_COLS = ATT_HEADS * 2 * ATT_QK_DIM
K_COLS = ATT_HEADS * 2 * ATT_QK_DIM
V_COLS = ATT_HEADS * ATT_V_DIM
GATE_COLS = N_BRANCH * D_MODEL
IN_COLS = Q_COLS + K_COLS + V_COLS + POOL_WIDTH + SSM_WIDTH + GATE_COLS
SPLITS = [Q_COLS, Q_COLS + K_COLS, Q_COLS + K_COLS + V_COLS,
          Q_COLS + K_COLS + V_COLS + POOL_WIDTH,
          Q_COLS + K_COLS + V_COLS + POOL_WIDTH + SSM_WIDTH]

kernel_name = "hybrid_diffattn_pool_s5_deepnorm"

def layer_norm(x, g, b):
    xf = x.astype(jnp.float32)
    mu = jnp.mean(xf, axis=-1, keepdims=True)
    var = jnp.mean(jnp.square(xf - mu), axis=-1, keepdims=True)
    return ((xf - mu) * lax.rsqrt(var + LN_EPS)).astype(x.dtype) * g + b

def rotary_tables(positions):
    inv_freq = ROPE_THETA ** (-jnp.arange(0, ROT_DIM, 2, dtype=jnp.float32) / ROT_DIM)
    ang = positions.astype(jnp.float32)[..., None] * inv_freq
    return jnp.cos(ang)[:, :, None, None, :], jnp.sin(ang)[:, :, None, None, :]

def apply_partial_rotary(t, cos, sin):
    half = ROT_DIM // 2
    tr = t[..., :ROT_DIM].astype(jnp.float32)
    t1, t2 = tr[..., :half], tr[..., half:]
    rot = jnp.concatenate([t1 * cos - t2 * sin, t2 * cos + t1 * sin], axis=-1).astype(t.dtype)
    return jnp.concatenate([rot, t[..., ROT_DIM:]], axis=-1)

def diff_attention(q, k, v, lam):
    bsz, s = q.shape[0], q.shape[1]
    nb = s // Q_BLOCK
    scale = 1.0 / math.sqrt(ATT_QK_DIM)
    k1, k2 = k[..., 0, :], k[..., 1, :]
    qb1 = jnp.moveaxis(q[..., 0, :].reshape(bsz, nb, Q_BLOCK, ATT_HEADS, ATT_QK_DIM), 1, 0)
    qb2 = jnp.moveaxis(q[..., 1, :].reshape(bsz, nb, Q_BLOCK, ATT_HEADS, ATT_QK_DIM), 1, 0)
    kpos = jnp.arange(s)
    neg = jnp.finfo(jnp.float32).min

    def block(args):
        i, a1, a2 = args
        qpos = i * Q_BLOCK + jnp.arange(Q_BLOCK)
        mask = (kpos[None, :] <= qpos[:, None])[None, None]
        s1 = jnp.einsum('bqhd,bkhd->bhqk', a1, k1).astype(jnp.float32) * scale
        s2 = jnp.einsum('bqhd,bkhd->bhqk', a2, k2).astype(jnp.float32) * scale
        p1 = jax.nn.softmax(jnp.where(mask, s1, neg), axis=-1)
        p2 = jax.nn.softmax(jnp.where(mask, s2, neg), axis=-1)
        attn = (p1 - lam * p2).astype(v.dtype)
        return jnp.einsum('bhqk,bkhd->bqhd', attn, v)

    out = lax.map(block, (jnp.arange(nb), qb1, qb2))
    return jnp.moveaxis(out, 0, 1).reshape(bsz, s, ATT_HEADS, ATT_V_DIM)

def multiscale_pool(u, w_pool, pool_scale):
    bsz, s, _ = u.shape
    uf = u.astype(jnp.float32).reshape(bsz, s, N_POOL, POOL_CH)
    cs0 = jnp.concatenate([jnp.zeros((bsz, 1, N_POOL, POOL_CH), jnp.float32),
                           jnp.cumsum(uf, axis=1)], axis=1)
    t = jnp.arange(s)
    outs = []
    for g, w in enumerate(POOL_WINDOWS):
        lo = jnp.pad(cs0[:, :, g], ((0, 0), (w - 1, 0), (0, 0)))[:, :s]
        cnt = jnp.minimum(t + 1, w).astype(jnp.float32)[None, :, None]
        outs.append((cs0[:, 1:, g] - lo) / cnt - uf[:, :, g])
    pooled = jnp.stack(outs, axis=2).astype(u.dtype)
    mixed = jnp.einsum('bsgc,gcd->bsgd', pooled, w_pool)
    return mixed.reshape(bsz, s, POOL_WIDTH) * pool_scale

def s5_ssm(u, a_re, a_im, log_dt, b_re, b_im, c_re, c_im, d_skip):
    f32 = jnp.float32
    bsz, s, _ = u.shape
    uf = u.astype(f32).reshape(bsz, s, SSM_GROUPS, SSM_GROUP_CH)
    ar, ai = a_re.astype(f32), a_im.astype(f32)
    dt = jnp.exp(log_dt.astype(f32))[:, None]
    mag = jnp.exp(ar * dt)
    ab_re, ab_im = mag * jnp.cos(ai * dt), mag * jnp.sin(ai * dt)
    den = ar * ar + ai * ai
    nr, ni = ab_re - 1.0, ab_im
    f_re = (nr * ar + ni * ai) / den
    f_im = (ni * ar - nr * ai) / den
    br, bi = b_re.astype(f32), b_im.astype(f32)
    bb_re = f_re[..., None] * br - f_im[..., None] * bi
    bb_im = f_re[..., None] * bi + f_im[..., None] * br
    bu_re = jnp.einsum('bsgh,gph->bsgp', uf, bb_re)
    bu_im = jnp.einsum('bsgh,gph->bsgp', uf, bb_im)
    a_re_t = jnp.broadcast_to(ab_re, bu_re.shape)
    a_im_t = jnp.broadcast_to(ab_im, bu_im.shape)

    def combine(e1, e2):
        a1r, a1i, b1r, b1i = e1
        a2r, a2i, b2r, b2i = e2
        return (a2r * a1r - a2i * a1i, a2r * a1i + a2i * a1r,
                a2r * b1r - a2i * b1i + b2r, a2r * b1i + a2i * b1r + b2i)

    _, _, xr, xi = lax.associative_scan(combine, (a_re_t, a_im_t, bu_re, bu_im), axis=1)
    y = (jnp.einsum('bsgp,ghp->bsgh', xr, c_re.astype(f32))
         - jnp.einsum('bsgp,ghp->bsgh', xi, c_im.astype(f32))
         + d_skip.astype(f32).reshape(SSM_GROUPS, SSM_GROUP_CH) * uf)
    return y.reshape(bsz, s, SSM_WIDTH).astype(u.dtype)

def setup_inputs(seed: int = 0) -> dict:
    key = jax.random.key(seed)
    ks = jax.random.split(key, 32)
    L = DEPTH

    def nrm(k, shape, scale):
        return jax.random.normal(k, shape, jnp.float32) * scale

    n_idx = jnp.arange(SSM_STATE, dtype=jnp.float32)
    return {
        "x": nrm(ks[0], (BATCH, SEQ, D_MODEL), 1.0),
        "positions": jnp.broadcast_to(jnp.arange(SEQ, dtype=jnp.int32)[None, :], (BATCH, SEQ)),
        "ln_in_g": 1.0 + nrm(ks[1], (D_MODEL,), 0.02),
        "ln_in_b": nrm(ks[2], (D_MODEL,), 0.02),
        "w_in": nrm(ks[3], (L, D_MODEL, IN_COLS), D_MODEL ** -0.5),
        "b_gate": nrm(ks[4], (L, GATE_COLS), 0.02),
        "lam_q1": nrm(ks[5], (L, ATT_QK_DIM), 0.1),
        "lam_k1": nrm(ks[6], (L, ATT_QK_DIM), 0.1),
        "lam_q2": nrm(ks[7], (L, ATT_QK_DIM), 0.1),
        "lam_k2": nrm(ks[8], (L, ATT_QK_DIM), 0.1),
        "subln_g": 1.0 + nrm(ks[9], (L, ATT_V_DIM), 0.02),
        "pool_w": nrm(ks[10], (L, N_POOL, POOL_CH, POOL_CH), POOL_CH ** -0.5),
        "pool_scale": 1.0 + nrm(ks[11], (L, POOL_WIDTH), 0.02),
        "ssm_a_re": -0.5 * jnp.exp(nrm(ks[12], (L, SSM_GROUPS, SSM_STATE), 0.01)),
        "ssm_a_im": math.pi * n_idx + nrm(ks[13], (L, SSM_GROUPS, SSM_STATE), 0.01),
        "ssm_log_dt": jax.random.uniform(ks[14], (L, SSM_GROUPS), jnp.float32,
                                         math.log(1e-3), math.log(1e-1)),
        "ssm_b_re": nrm(ks[15], (L, SSM_GROUPS, SSM_STATE, SSM_GROUP_CH), (2.0 * SSM_GROUP_CH) ** -0.5),
        "ssm_b_im": nrm(ks[16], (L, SSM_GROUPS, SSM_STATE, SSM_GROUP_CH), (2.0 * SSM_GROUP_CH) ** -0.5),
        "ssm_c_re": nrm(ks[17], (L, SSM_GROUPS, SSM_GROUP_CH, SSM_STATE), 0.5),
        "ssm_c_im": nrm(ks[18], (L, SSM_GROUPS, SSM_GROUP_CH, SSM_STATE), 0.5),
        "ssm_d": nrm(ks[19], (L, SSM_WIDTH), 1.0),
        "glu_w": nrm(ks[20], (L, SSM_WIDTH, SSM_WIDTH), SSM_WIDTH ** -0.5),
        "glu_b": nrm(ks[21], (L, SSM_WIDTH), 0.02),
        "proj_attn": nrm(ks[22], (L, ATT_WIDTH, D_MODEL), ATT_WIDTH ** -0.5),
        "proj_pool": nrm(ks[23], (L, POOL_WIDTH, D_MODEL), POOL_WIDTH ** -0.5),
        "proj_ssm": nrm(ks[24], (L, SSM_WIDTH, D_MODEL), SSM_WIDTH ** -0.5),
        "w_out": nrm(ks[25], (L, D_MODEL, D_MODEL), DEEPNORM_BETA * D_MODEL ** -0.5),
        "ln1_g": 1.0 + nrm(ks[26], (L, D_MODEL), 0.02),
        "ln1_b": nrm(ks[27], (L, D_MODEL), 0.02),
        "w_up": nrm(ks[28], (L, D_MODEL, D_FF), D_MODEL ** -0.5),
        "w_down": nrm(ks[29], (L, D_FF, D_MODEL), DEEPNORM_BETA * D_FF ** -0.5),
        "ln2_g": 1.0 + nrm(ks[30], (L, D_MODEL), 0.02),
        "ln2_b": nrm(ks[31], (L, D_MODEL), 0.02),
    }

def reference(x, positions, ln_in_g, ln_in_b, w_in, b_gate, lam_q1, lam_k1, lam_q2, lam_k2,
              subln_g, pool_w, pool_scale, ssm_a_re, ssm_a_im, ssm_log_dt, ssm_b_re, ssm_b_im,
              ssm_c_re, ssm_c_im, ssm_d, glu_w, glu_b, proj_attn, proj_pool, proj_ssm, w_out,
              ln1_g, ln1_b, w_up, w_down, ln2_g, ln2_b):
    bsz, s, _ = x.shape
    h = layer_norm(x, ln_in_g, ln_in_b)
    cos, sin = rotary_tables(positions)
    for l in range(DEPTH):
        lam_init = 0.8 - 0.6 * math.exp(-0.3 * l)
        proj = h @ w_in[l]
        q, k, v, u_pool, u_ssm, g = jnp.split(proj, SPLITS, axis=-1)
        gates = jax.nn.sigmoid(g + b_gate[l]).reshape(bsz, s, N_BRANCH, D_MODEL)

        q = apply_partial_rotary(q.reshape(bsz, s, ATT_HEADS, 2, ATT_QK_DIM), cos, sin)
        k = apply_partial_rotary(k.reshape(bsz, s, ATT_HEADS, 2, ATT_QK_DIM), cos, sin)
        v = v.reshape(bsz, s, ATT_HEADS, ATT_V_DIM)
        f32 = jnp.float32
        lam = (jnp.exp(jnp.sum(lam_q1[l].astype(f32) * lam_k1[l].astype(f32)))
               - jnp.exp(jnp.sum(lam_q2[l].astype(f32) * lam_k2[l].astype(f32))) + lam_init)
        o = diff_attention(q, k, v, lam)
        of = o.astype(f32)
        o = (of * lax.rsqrt(jnp.mean(of * of, axis=-1, keepdims=True) + LN_EPS)).astype(x.dtype)
        y_attn = (o * subln_g[l] * (1.0 - lam_init)).reshape(bsz, s, ATT_WIDTH)

        y_pool = multiscale_pool(u_pool, pool_w[l], pool_scale[l])

        y_s = jax.nn.gelu(s5_ssm(u_ssm, ssm_a_re[l], ssm_a_im[l], ssm_log_dt[l], ssm_b_re[l],
                                 ssm_b_im[l], ssm_c_re[l], ssm_c_im[l], ssm_d[l]))
        y_ssm = y_s * jax.nn.sigmoid(y_s @ glu_w[l] + glu_b[l])

        merged = (gates[:, :, 0] * (y_attn @ proj_attn[l])
                  + gates[:, :, 1] * (y_pool @ proj_pool[l])
                  + gates[:, :, 2] * (y_ssm @ proj_ssm[l]))
        h = layer_norm(DEEPNORM_ALPHA * h + merged @ w_out[l], ln1_g[l], ln1_b[l])

        ff = jnp.square(jax.nn.relu(h @ w_up[l])) @ w_down[l]
        h = layer_norm(DEEPNORM_ALPHA * h + ff, ln2_g[l], ln2_b[l])
    return h


_drawn_inputs = setup_inputs


def setup_inputs(seed=0):
    import zlib

    import numpy as np

    out = dict(_drawn_inputs(seed))
    spreads = {}
    factors = {'b_gate': 8.0,
     'lam_q1': 3.933,
     'lam_q2': 2.896,
     'lam_k2': 4.32,
     'subln_g': 25.33,
     'pool_scale': 22.444,
     'ssm_a_re': 200.0,
     'glu_b': 200.0,
     'ssm_a_im': 64.0,
     'ssm_log_dt': 64.0,
     'ssm_b_re': 64.0,
     'ssm_b_im': 64.0,
     'ssm_c_re': 64.0,
     'ssm_c_im': 64.0,
     'glu_w': 16.597}
    for name, (base, spread) in spreads.items():
        noise = np.random.default_rng([zlib.crc32(name.encode()), seed]).standard_normal(out[name].shape)
        drawn = base * np.exp(spread * noise) if base else spread * noise
        out[name] = __import__('jax').numpy.asarray(drawn.astype(out[name].dtype))
    for name, factor in factors.items():
        out[name] = (out[name] * factor).astype(out[name].dtype)
    return out
```

```python
import math

import numpy as np
import concourse.bass as bass
from concourse import mybir
from contextlib import ExitStack

D_MODEL = 2048
SEQ = 256
DEPTH = 2
HEADS = 8
QK = 64
ROT = QK // 4
ROPE_THETA = 500000.0
POOL_WINDOWS = (2, 4, 8, 16)
SSM_WIDTH = 512
SSM_CH = 16
SSM_STATE = 64
D_FF = 4 * D_MODEL
IN_COLS = 3 * HEADS * 2 * QK + 2 * SSM_WIDTH + 3 * D_MODEL
ALPHA = (2.0 * DEPTH) ** 0.25
LN_EPS = 1e-5

P = 128
TT = SEQ // P
NS = 512
KT = D_MODEL // P
CK = 2
CPS = KT // CK
RING = 4
AHEAD = 2
FREE = 1
NSL = D_MODEL // NS
FF_GROUPS = D_FF // D_MODEL
GATE0 = IN_COLS - 3 * D_MODEL
POOL0 = 3 * HEADS * 2 * QK
SSM0 = POOL0 + SSM_WIDTH
PAIRS = SSM_WIDTH // (2 * SSM_CH)
PPT = P // (2 * SSM_CH)
CT = SSM_WIDTH // P

C_WIN = 0
C_GATE = 8 * CPS
C_PROJ = C_GATE + 12 * CPS
C_WOUT = C_PROJ + NSL * CPS
C_MLP = C_WOUT + NSL * CPS
C_LAYER = C_MLP + FF_GROUPS * 2 * NSL * CPS
G_GATE = (4, 4)
G_PROJ = (G_GATE[0] + 8, G_GATE[1] + 4)
G_WOUT = (G_PROJ[0] + 6, G_PROJ[1] + 6)
G_MLP = (G_WOUT[0] + 2, G_WOUT[1] + 2)
G_LAYER = (G_MLP[0] + 16, G_MLP[1] + 16)
U_MERGE = 0
U_LN1 = 8
U_MLP = 16
U_LN2 = U_MLP + 8 * FF_GROUPS
U_LAYER = U_LN2 + 8

MASKED = -(2.0 ** 100)
MAGIC = 1.5 * 2.0 ** 23
PI2_1 = 6.28125
PI2_2 = float(np.float32(2 * math.pi - PI2_1) - np.float32(0)) if False else 0.0019350051879882812
PI2_3 = 2 * math.pi - PI2_1 - PI2_2
GELU_C = math.sqrt(2.0 / math.pi)

PC_AR, PC_AI, PC_LDT = 0, PAIRS, 2 * PAIRS
PC_D = 3 * PAIRS
PC_GLUB = PC_D + CT
PC_PSC = PC_GLUB + CT
PC_SUBG = PC_PSC + CT
PC_LAMC = PC_SUBG + 1
PC_LAM = PC_LAMC + 2
PC_N = PC_LAM + 4 * QK
CC_IDENT = 0
CC_MASK = P
CC_MT = 2 * P
CC_FREQ = CC_MT + 12 * P
CC_N = CC_FREQ + ROT // 2


def build_trunk(nc, x, pos, ln_in, w_in, b_gate, colp, pool_w, ssm_bc, glu_w, proj_attn, proj_pool, proj_ssm,
                w_out, ln1, w_up, w_down, ln2, consts, gates_dram, out):
    F32, FR, I32 = mybir.dt.float32, mybir.dt.float32r, mybir.dt.int32
    ALU, ACT, AX = mybir.AluOpType, mybir.ActivationFunctionType, mybir.AxisListType
    ctx = ExitStack()
    with ctx:
        def sb(name, shape, dt=F32):
            return ctx.enter_context(nc.sbuf_tensor(name, shape, dt))

        def sem(name):
            return ctx.enter_context(nc.semaphore(name))

        raw = sb("raw", [P, RING, CK, NS])
        whi = sb("whi", [P, RING, CK, NS], FR)
        wlo = sb("wlo", [P, RING, CK, NS], FR)
        aT = [sb("aT_hi", [P, KT, SEQ], FR), sb("aT_lo", [P, KT, SEQ], FR)]
        yT = [sb("yT_hi", [P, KT, SEQ], FR), sb("yT_lo", [P, KT, SEQ], FR)]
        h = sb("h", [P, TT, D_MODEL])
        qk = sb("qk", [P, 2 * HEADS, SEQ])
        lnp = qk[:, :, :].rearrange("p a b -> p (a b)").rearrange("p (a n) -> p a n", a=2)
        v = sb("v", [P, TT, HEADS * P])
        gluw = v[:, :, :].rearrange("p a b -> p (a b)").rearrange("p (k n) -> p k n", k=CT)
        uT = sb("uT", [P, CT, SEQ])
        stg = sb("stg", [P, 2, TT, NS])
        merged = sb("merged", [P, TT, NS])
        rot = sb("rot", [P, 2, PPT, SEQ])
        rtmp = sb("rtmp", [P, PPT, P])
        pq = sb("pq", [P, 4, SEQ])
        rr = sb("rr", [P, 2, SEQ])
        gl = sb("gl", [P, 2, SEQ])
        ex = sb("ex", [P, 2, 2, SEQ])
        ats = sb("ats", [P, 3 * P])
        atT = sb("atT", [P, 3 * P])
        osb = sb("osb", [P, 2, P])
        junk = sb("junk", [P, P])
        qs = sb("qs", [P, 2, SEQ])
        bc = sb("bc", [P, 4, P])
        cf = sb("cf", [P, 2, P])
        poolw = sb("poolw", [P, CT, P])
        biasb = sb("biasb", [P, NS])
        cst = sb("cst", [P, CC_N])
        ident = cst[:, CC_IDENT:CC_IDENT + P]
        mask = cst[:, CC_MASK:CC_MASK + P]
        mt = cst[:, CC_MT:CC_MT + 12 * P].rearrange("p (g b n) -> p g b n", g=4, b=3)
        cp = sb("cp", [P, PC_N])
        posi = sb("posi", [P, TT], I32)
        rope = sb("rope", [P, 2, TT, ROT // 2])
        rt = sb("rt", [P, 4, TT, 8, ROT // 2])
        sm = sb("sm", [P, 16, 16])
        pw = sb("pw", [P, 8, 2, 16])
        ff = sb("ff", [P, 2, 16])
        halfc = sb("halfc", [P, 4, 16])
        stats = sb("stats", [P, TT, NSL, 6])
        mv = sb("mv", [P, TT, 2])
        rstd = sb("rstd", [P, TT])
        mx = sb("mx", [P, 2, 2])
        sums = sb("sums", [P, 2, 2])
        rc = sb("rc", [P, 2, 2])
        ss = sb("ss", [P, 2])
        rms = sb("rms", [P, 2])
        lamt = sb("lamt", [P, 2 * QK])
        lam = sb("lam", [P, 4])
        subg = sb("subg", [P, 1])
        glubh = sb("glubh", [P, CT])

        acc = [ctx.enter_context(nc.psum_tensor(f"acc{i}", [P, TT, NS], F32)) for i in range(2)]
        S = [ctx.enter_context(nc.psum_tensor(f"side{i}", [P, NS], F32)) for i in range(4)]

        raw_arrived = [sem(f"raw_arrived{i}") for i in range(RING)]
        hi_ready = [sem(f"hi_ready{i}") for i in range(RING)]
        lo_ready = [sem(f"lo_ready{i}") for i in range(RING)]
        chunk_used = [sem(f"chunk_used{i}") for i in range(RING)]
        acc_free = [sem(f"acc_free{i}") for i in range(2)]
        t_src, t_bank, t_hi, t_lo = sem("t_src"), sem("t_bank"), sem("t_hi"), sem("t_lo")
        x_bank, x_out, rope_done = sem("x_bank"), sem("x_out"), sem("rope_done")
        ln_var, ln_rstd, lnp_arrived, h_scaled, h_final = (sem("ln_var"), sem("ln_rstd"), sem("lnp_arrived"),
                                                           sem("h_scaled"), sem("h_final"))
        x_arrived, cst_arrived, cp_arrived, bc_arrived, glu_arrived = (sem("x_arrived"), sem("cst_arrived"),
                                                                       sem("cp_arrived"), sem("bc_arrived"), sem("glu_arrived"))
        bias_arrived, bias_used, out_stored = sem("bias_arrived"), sem("bias_used"), sem("out_stored")
        stg_stored = [sem(f"stg_stored{i}") for i in range(2)]
        gate_arrived = [sem(f"gate_arrived{i}") for i in range(2)]
        gate_tanh, merge_done = sem("gate_tanh"), sem("merge_done")
        ang_done, sin_done, params_done = sem("ang_done"), sem("sin_done"), sem("params_done")
        p_mean, p_copy, p_mix, p_hi, p_lo = sem("p_mean"), sem("p_copy"), sem("p_mix"), sem("p_hi"), sem("p_lo")
        (q_copied, score_done, max_done, exp_done, at_done, atT_done, atT_copied, pv_done, ss_done, rms_done, o_done,
         oT_done, o_hi, o_lo) = [sem(n) for n in (
             "q_copied", "score_done", "max_done", "exp_done", "at_done", "atT_done", "atT_copied", "pv_done",
             "ss_done", "rms_done", "o_done", "oT_done", "o_hi", "o_lo")]
        u_copied, bu_done, pq_done, r_done, xx_done = (sem("u_copied"), sem("bu_done"), sem("pq_done"), sem("r_done"),
                                                       sem("xx_done"))
        tab_done, cf_done, y_done, gelu_in, gelu_tanh, y2_done = (sem("tab_done"), sem("cf_done"), sem("y_done"),
                                                                  sem("gelu_in"), sem("gelu_tanh"), sem("y2_done"))
        glu_mm, glu_tanh, glu_prod, glu_hi, glu_lo = (sem("glu_mm"), sem("glu_tanh"), sem("glu_prod"),
                                                      sem("glu_hi"), sem("glu_lo"))

        def slot(turn, j):
            return turn + j // RING, j % RING

        def finished(eng, turn, j):
            t, s = slot(turn, j)
            eng.wait_ge(chunk_used[s], t + 1 + FREE)

        def wait_alone(eng, what, value):
            value = value if isinstance(value, int) else eng.to_reg(value)
            eng.wait_ge(cst_arrived, 32)
            eng.wait_ge(what, value)

        lay = C_LAYER // RING
        block = ctx.enter_context(nc.Block())

        @block.sync
        def _(sp):
            def load(turn, j, w, li, k0, n0):
                t, s = slot(turn, j)
                wait_alone(sp, lo_ready[s], t + FREE)
                src = w[bass.ds(li, 1), bass.ds(k0, CK * P), bass.ds(n0, NS)]
                sp.dma_start(raw[:, s], src.rearrange("o (t p) n -> p (o t) n", p=P)).then_inc(raw_arrived[s], 16)

            def load_norm(g, b):
                sp.dma_start(lnp[:, 0, :], g).then_inc(lnp_arrived, 16)
                sp.dma_start(lnp[:, 1, :], b).then_inc(lnp_arrived, 16)

            for t in range(TT):
                sp.dma_start(h[:, t, :], x[t * P:(t + 1) * P, :]).then_inc(x_arrived, 16)
            load_norm(ln_in[0:1, :].to_broadcast([P, D_MODEL]), ln_in[1:2, :].to_broadcast([P, D_MODEL]))
            sp.dma_start(cst[:, :], consts).then_inc(cst_arrived, 16)
            sp.dma_start(posi[:, :], pos).then_inc(cst_arrived, 16)
            with sp.Fori(0, DEPTH) as li:
                turn = li * lay
                wait_alone(sp, h_scaled, li + FREE)
                sp.dma_start(cp[:, :], colp[bass.ds(li, 1)].rearrange("o p n -> (o p) n")).then_inc(cp_arrived, 16)
                sp.dma_start(poolw[:, :, :], pool_w[bass.ds(li, 1)].rearrange("o g c d -> c (o g) d"))\
                    .then_inc(cp_arrived, 16)
                for r, n0 in enumerate((SSM0, POOL0, 0, NS, 2 * NS, 3 * NS, 4 * NS, 5 * NS)):
                    for j in range(CPS):
                        load(turn + r * 2, j, w_in, li, j * CK * P, n0)
                with sp.Fori(0, CT) as i:
                    for s in range(3):
                        for j in range(CPS):
                            load(turn + C_GATE // RING + i * 6, s * CPS + j, w_in, li, j * CK * P,
                                 GATE0 + i * (3 * NS) + s * NS)
                            if s == 0 and j == 3:
                                wait_alone(sp, bu_done, li * PAIRS + i * PPT + FREE)
                                wait_alone(sp, cf_done, li * CT + i + FREE)
                                sp.dma_start(bc[:, :, :], ssm_bc[bass.ds(li, 1), bass.ds(i, 1)]
                                             .rearrange("o u p a n -> p (o u a) n")).then_inc(bc_arrived, 16)
                            if j == 6:
                                wait_alone(sp, bias_used, li * 12 + i * 3 + s + FREE)
                                sp.dma_start(biasb[:, :], b_gate[bass.ds(li, 1), bass.ds(i * (3 * NS) + s * NS, NS)]
                                             .to_broadcast([P, NS])).then_inc(bias_arrived, 16)
                for n in range(NSL):
                    for j in range(CPS):
                        w, k0 = ((proj_attn, j * CK * P) if j < 4 else
                                 (proj_pool, (j - 4) * CK * P) if j < 6 else (proj_ssm, (j - 6) * CK * P))
                        load(turn + C_PROJ // RING + n * 2, j, w, li, k0, n * NS)
                        if n == 0 and j == 0:
                            wait_alone(sp, pv_done, (li + 1) * HEADS)
                            sp.dma_start(gluw, glu_w[bass.ds(li, 1)].rearrange("o (k p) n -> p (o k) n", p=P))\
                                .then_inc(glu_arrived, 16)
                        if n == 2 and j == 0:
                            wait_alone(sp, score_done, (li + 1) * HEADS)
                            load_norm(ln1[bass.ds(li, 1), 0:1, :].rearrange("o a n -> (o a) n").to_broadcast([P, D_MODEL]),
                                      ln1[bass.ds(li, 1), 1:2, :].rearrange("o a n -> (o a) n").to_broadcast([P, D_MODEL]))
                for n in range(NSL):
                    for j in range(CPS):
                        load(turn + C_WOUT // RING + n * 2, j, w_out, li, j * CK * P, n * NS)
                with sp.Fori(0, FF_GROUPS) as g:
                    for n in range(NSL):
                        for j in range(CPS):
                            load(turn + C_MLP // RING + g * 16 + n * 2, j, w_up, li, j * CK * P, g * D_MODEL + n * NS)
                    for n in range(NSL):
                        for j in range(CPS):
                            load(turn + C_MLP // RING + g * 16 + 8 + n * 2, j, w_down, li,
                                 g * D_MODEL + j * CK * P, n * NS)
                wait_alone(sp, h_scaled, li + 1 + FREE)
                load_norm(ln2[bass.ds(li, 1), 0:1, :].rearrange("o a n -> (o a) n").to_broadcast([P, D_MODEL]),
                          ln2[bass.ds(li, 1), 1:2, :].rearrange("o a n -> (o a) n").to_broadcast([P, D_MODEL]))
            for j in range(AHEAD):
                load(DEPTH * lay, j, w_in, 0, j * CK * P, SSM0)
            sp.wait_ge(h_final, 1)
            for t in range(TT):
                sp.dma_start(out[t * P:(t + 1) * P, :], h[:, t, :]).then_inc(out_stored, 16)
            sp.wait_ge(out_stored, 16 * TT)

        @block.scalar
        def _(act):
            def split_hi(turn, j):
                t, s = slot(turn, j)
                act.wait_ge(raw_arrived[s], (t + 1) * 16)
                act.wait_ge(chunk_used[s], t + FREE)
                nc.scalar.activation(whi[:, s], raw[:, s], ACT.Copy).then_inc(hi_ready[s], 1)

            def t_unit(u, par, dst, kt0, tt, scale=1.0):
                act.wait_ge(t_bank, u + 1)
                nc.scalar.activation(dst[0][:, kt0:kt0 + 4, tt * P:(tt + 1) * P],
                                     S[par][:, :].rearrange("p (k n) -> p k n", k=4), ACT.Copy, scale=scale)\
                    .then_inc(t_hi, 1)

            def t_units(u0, dst, kt0, scale=1.0):
                for tt in range(TT):
                    t_unit(u0 + tt, tt, dst, kt0, tt, scale)

            def ln_units(u0):
                for q in range(NSL):
                    t_units(u0 + 2 * q, aT, 4 * q)

            def head_step(st, hn, hd):
                if st == 0:
                    nc.scalar.activation(qs[:, :, :], qk[:, :, :].rearrange("p (a h) n -> p a h n", a=2)[:, :, bass.ds(hd, 1), :]
                                         .rearrange("p a h n -> p a (h n)"), ACT.Copy)\
                        .then_inc(q_copied, 1)
                elif st == 1:
                    act.wait_ge(max_done, hn + 1)
                    for qt in range(2):
                        for c in range(2):
                            w = (qt + 1) * P
                            i_ = nc.scalar.activation(ex[:, qt, c, 0:w], S[c][:, qt * P:qt * P + w], ACT.Exp,
                                                      scale=QK ** -0.5, bias=mx[:, qt, c:c + 1],
                                                      accum_out=sums[:, qt, c:c + 1])
                    i_.then_inc(exp_done, 1)
                elif st == 3:
                    act.wait_ge(atT_done, hn + 1)
                    nc.scalar.activation(atT[:, :], S[0][:, 0:3 * P], ACT.Copy).then_inc(atT_copied, 1)
                elif st == 4:
                    act.wait_ge(pv_done, hn + 1)
                    for qt in range(2):
                        if qt:
                            act.drain()
                        i_ = nc.scalar.activation(junk[:, :], S[1][:, qt * P:(qt + 1) * P], ACT.Square,
                                                  accum_out=ss[:, qt:qt + 1])
                    i_.then_inc(ss_done, 1)
                elif st == 6:
                    act.wait_ge(oT_done, hn + 1)
                    nc.scalar.activation(yT[0][:, bass.ds(hd, 1), :].rearrange("p a n -> p (a n)"), S[0][:, 0:SEQ],
                                         ACT.Copy, scale=subg[:, 0:1]).then_inc(o_hi, 1)

            for x_ in (acc_free[0], acc_free[1], x_out):
                act.sem_inc(x_, FREE)
            for x_ in stg_stored:
                act.sem_inc(x_, 16 * FREE)
            act.wait_ge(ang_done, 1)
            for k in range(2):
                i_ = nc.scalar.activation(rope[:, k].rearrange("p t n -> p (t n)"), sm[:, k, :], ACT.Sin)
            i_.then_inc(sin_done, 1)
            ln_units(0)
            for j in range(AHEAD):
                split_hi(0, j)
            with act.Fori(0, DEPTH) as li:
                turn = li * lay
                for r in range(8):
                    tr = turn + 2 * r
                    for j in range(CPS):
                        split_hi(tr, j + AHEAD)
                        if j == 2 and (r == 1 or 3 <= r <= 6):
                            xu = li * 10 + (8 if r == 1 else 2 * (r - 3)) if r != 1 else li * 10
                            xu = li * 10 + (0 if r == 1 else 2 * (r - 2))
                            for tt in range(TT):
                                act.wait_ge(x_bank, xu + tt + 1)
                                dst = uT if r == 1 else qk
                                k0 = 0 if r == 1 else 4 * (r - 3)
                                nc.scalar.activation(dst[:, k0:k0 + 4, tt * P:(tt + 1) * P],
                                                     S[2 + tt][:, :].rearrange("p (k n) -> p k n", k=4), ACT.Copy)\
                                    .then_inc(x_out, 1)
                        if r == 2 and j == 2:
                            act.wait_ge(p_mean, li + 1)
                            for b in range(2):
                                i_ = nc.scalar.activation(pq[:, 2 * b:2 * b + 2, :],
                                                          S[2 + b][:, :].rearrange("p (g n) -> p g n", g=2), ACT.Copy)
                            i_.then_inc(p_copy, 1)
                        if r == 2 and j == 4:
                            act.wait_ge(p_mix, li + 1)
                            for g in range(CT):
                                i_ = nc.scalar.activation(yT[0][:, 8 + g, :], S[2 + g // 2][:, (g % 2) * SEQ:(g % 2 + 1) * SEQ],
                                                          ACT.Copy, scale=cp[:, PC_PSC + g:PC_PSC + g + 1])
                            i_.then_inc(p_hi, 1)
                        if r == 4 and j == 5:
                            act.wait_ge(ang_done, li + 2)
                            for k in range(2):
                                i_ = nc.scalar.activation(sm[:, 2 + k, :], sm[:, k, :], ACT.Sin)
                            i_.then_inc(sin_done, 1)
                    finished(act, tr, CPS - 1)
                    if r < 6:
                        nc.scalar.activation(stg[:, r % 2], acc[r % 2][:, :, :], ACT.Copy).then_inc(acc_free[r % 2], 1)
                    else:
                        nc.scalar.activation(v[:, :, (r - 6) * NS:(r - 5) * NS], acc[r % 2][:, :, :], ACT.Copy)\
                            .then_inc(acc_free[r % 2], 1)
                with act.Fori(0, CT) as i:
                    tg = turn + C_GATE // RING + i * 6
                    for j in range(3 * CPS):
                        split_hi(tg, j + AHEAD)
                        for hh in range(2):
                            if 0 <= j - 12 * hh <= 6:
                                head_step(j - 12 * hh, li * HEADS + i * 2 + hh, i * 2 + hh)
                        if j == 7:
                            nc.scalar.activation(gl[:, 0, :], uT[:, bass.ds(i, 1), :].rearrange("p a n -> p (a n)"),
                                                 ACT.Copy).then_inc(u_copied, 1)
                        if j == 22:
                            act.wait_ge(gelu_in, li * CT + i + 1)
                            nc.scalar.activation(gl[:, 1, :], gl[:, 1, :], ACT.Tanh, scale=GELU_C).then_inc(gelu_tanh, 1)
                        if j % CPS == CPS - 1:
                            s = j // CPS
                            b = s % 2
                            n_free = (li * G_LAYER[b] + i * (2, 1)[b]) + (G_GATE[b] + s // 2 + 1)
                            act.wait_ge(acc_free[b], n_free + FREE)
                            nc.scalar.activation(stg[:, b], stg[:, b], ACT.Tanh, scale=0.5).then_inc(gate_tanh, 1)
                            act.wait_ge(gate_tanh, li * 12 + i * 3 + s + 1)
                            act.dma_start(gates_dram[:, :, bass.ds(i * (3 * NS) + s * NS, NS)].rearrange("t p n -> p t n"),
                                          stg[:, b]).then_inc(stg_stored[b], 16)
                for n in range(NSL):
                    tp = turn + C_PROJ // RING + 2 * n
                    for j in range(CPS):
                        split_hi(tp, j + AHEAD)
                        if j in (0, 4, 6):
                            br = (0, 4, 6).index(j)
                            q = 3 * n + br
                            if q < 2:
                                for b in range(2):
                                    act.wait_ge(stg_stored[b], (li + 1) * 16 * (8, 4)[b] + 16 * FREE)
                            else:
                                act.wait_ge(merge_done, li * 12 + q - 1)
                            act.dma_start(stg[:, q % 2], gates_dram[:, :, br * D_MODEL + n * NS:br * D_MODEL + (n + 1) * NS]
                                          .rearrange("t p n -> p t n")).then_inc(gate_arrived[q % 2], 16)
                        if n == 0 and j == 1:
                            for ot in range(CT):
                                act.wait_ge(glu_mm, li * 2 + ot // 2 + 1)
                                i_ = nc.scalar.activation(ex[:, ot // 2, ot % 2, :], S[2 + ot // 2][:, (ot % 2) * SEQ:(ot % 2 + 1) * SEQ],
                                                          ACT.Tanh, scale=0.25, bias=glubh[:, ot:ot + 1])
                            i_.then_inc(glu_tanh, 1)
                        if n == 0 and j == 2:
                            act.wait_ge(glu_prod, li + 1)
                            nc.scalar.activation(yT[0][:, 12:16, :], ex[:, :, :, :].rearrange("p a b n -> p (a b) n"),
                                                 ACT.Copy, scale=0.25).then_inc(glu_hi, 1)
                        if n > 0 and j == 2:
                            t_units(8 + li * U_LAYER + U_MERGE + 2 * (n - 1), aT, 4 * (n - 1), 0.5)
                for n in range(NSL):
                    tw = turn + C_WOUT // RING + 2 * n
                    for j in range(CPS):
                        split_hi(tw, j + AHEAD)
                        if n == 0 and j == 2:
                            t_units(8 + li * U_LAYER + U_MERGE + 6, aT, 12, 0.5)
                ln_units(8 + li * U_LAYER + U_LN1)
                with act.Fori(0, FF_GROUPS) as g:
                    tm = turn + C_MLP // RING + g * 16
                    um = 8 + li * U_LAYER + U_MLP + g * 8
                    for n in range(NSL):
                        for j in range(CPS):
                            split_hi(tm + 2 * n, j + AHEAD)
                            if n > 0 and j == 2:
                                t_units(um + 2 * (n - 1), yT, 4 * (n - 1))
                        finished(act, tm + 2 * n, CPS - 1)
                        nc.scalar.activation(stg[:, n % 2], acc[n % 2][:, :, :], ACT.Relu).then_inc(acc_free[n % 2], 1)
                        act.drain()
                        nc.scalar.activation(stg[:, n % 2], stg[:, n % 2], ACT.Square).then_inc(t_src, 2)
                    for n in range(NSL):
                        for j in range(CPS):
                            split_hi(tm + 8 + 2 * n, j + AHEAD)
                            if n == 0 and j == 2:
                                t_units(um + 6, yT, 12)
                ln_units(8 + li * U_LAYER + U_LN2)

        @block.vector
        def _(dve):
            def split_lo(turn, j):
                t, s = slot(turn, j)
                dve.wait_ge(hi_ready[s], t + 1)
                nc.vector.tensor_tensor(wlo[:, s], raw[:, s], whi[:, s].bitcast(F32), ALU.subtract)\
                    .then_inc(lo_ready[s], 1)

            def t_unit(u, par, dst, kt0, tt, scale):
                dve.wait_ge(t_hi, u + 1)
                lo = dst[1][:, kt0:kt0 + 4, tt * P:(tt + 1) * P]
                hi = dst[0][:, kt0:kt0 + 4, tt * P:(tt + 1) * P].bitcast(F32)
                bank = S[par][:, :].rearrange("p (k n) -> p k n", k=4)
                if scale == 1.0:
                    nc.vector.tensor_tensor(lo, bank, hi, ALU.subtract).then_inc(t_lo, 1)
                else:
                    nc.vector.scalar_tensor_tensor(out=lo, in0=bank, scalar=scale, in1=hi, op0=ALU.mult,
                                                   op1=ALU.subtract).then_inc(t_lo, 1)

            def t_units(u0, dst, kt0, scale=1.0):
                for tt in range(TT):
                    t_unit(u0 + tt, tt, dst, kt0, tt, scale)

            def layer_norm(q, u0):
                dve.drain()
                for tt in range(TT):
                    i_ = nc.vector.bn_aggr(mv[:, tt, :], stats[:, tt].rearrange("p a b -> p (a b)"))
                i_.then_inc(ln_var, 1)
                dve.wait_ge(ln_rstd, q + 1)
                for tt in range(TT):
                    nc.vector.tensor_scalar(h[:, tt, :], h[:, tt, :], mv[:, tt, 0:1], rstd[:, tt:tt + 1],
                                            ALU.subtract, ALU.mult)
                wait_alone(dve, lnp_arrived, (q + 1) * 32)
                dve.drain()
                for qq in range(NSL):
                    c = slice(qq * NS, (qq + 1) * NS)
                    for tt in range(TT):
                        nc.vector.tensor_tensor(h[:, tt, c], h[:, tt, c], lnp[:, 0, c], ALU.mult)
                    dve.drain()
                    for tt in range(TT):
                        nc.vector.tensor_tensor(h[:, tt, c], h[:, tt, c], lnp[:, 1, c], ALU.add).then_inc(t_src, 1)
                    if qq > 0:
                        t_units(u0 + 2 * (qq - 1), aT, 4 * (qq - 1))
                t_units(u0 + 6, aT, 12)

            def statistics(n):
                for tt in range(TT):
                    nc.vector.bn_stats(stats[:, tt, n, :], h[:, tt, n * NS:(n + 1) * NS])

            def head_step(st, hn, hd):
                if st == 1:
                    dve.wait_ge(score_done, hn + 1)
                    for qt in range(2):
                        for c in range(2):
                            nc.vector.reduce_max(rc[:, qt, c:c + 1], S[c][:, qt * P:(2 * qt + 1) * P], AX.X)
                    dve.drain()
                    nc.vector.tensor_scalar(mx[:, :, :], rc[:, :, :], -(QK ** -0.5), None, ALU.mult)\
                        .then_inc(max_done, 1)
                elif st == 2:
                    dve.wait_ge(exp_done, hn + 1)
                    nc.vector.reciprocal(rc[:, :, :], sums[:, :, :])
                    dve.drain()
                    nc.vector.tensor_scalar(mx[:, :, 1:2], rc[:, :, 1:2], lam[:, 3:4], None, ALU.mult)
                    dve.drain()
                    for qt in range(2):
                        nc.vector.tensor_scalar(ex[:, qt, 1, 0:(qt + 1) * P], ex[:, qt, 1, 0:(qt + 1) * P],
                                                mx[:, qt, 1:2], None, ALU.mult)
                    dve.drain()
                    for qt in range(2):
                        i_ = nc.vector.scalar_tensor_tensor(
                            out=ats[:, qt * P:(2 * qt + 1) * P], in0=ex[:, qt, 0, 0:(qt + 1) * P],
                            scalar=rc[:, qt, 0:1], in1=ex[:, qt, 1, 0:(qt + 1) * P], op0=ALU.mult, op1=ALU.add)
                    i_.then_inc(at_done, 1)
                elif st == 5:
                    dve.wait_ge(rms_done, hn + 1)
                    for qt in range(2):
                        i_ = nc.vector.tensor_scalar(osb[:, qt, :], S[1][:, qt * P:(qt + 1) * P], rms[:, qt:qt + 1], None,
                                                     ALU.mult)
                    i_.then_inc(o_done, 1)
                elif st == 6:
                    dve.wait_ge(o_hi, hn + 1)
                    nc.vector.scalar_tensor_tensor(
                        out=yT[1][:, bass.ds(hd, 1), :].rearrange("p a n -> p (a n)"), in0=S[0][:, 0:SEQ],
                        scalar=subg[:, 0:1], in1=yT[0][:, bass.ds(hd, 1), :].rearrange("p a n -> p (a n)").bitcast(F32),
                        op0=ALU.mult, op1=ALU.subtract).then_inc(o_lo, 1)

            def pair_step(st, pn, pi, pp, tn):
                co = rot[:, 0, pp, :].unsqueeze(1).to_broadcast([P, 2, SEQ])
                si = rot[:, 1, pp, :].unsqueeze(1).to_broadcast([P, 2, SEQ])
                if st == 0:
                    if pp == 0:
                        dve.wait_ge(tab_done, tn + 1)
                    dve.wait_ge(bu_done, pn + 1 + FREE)
                    dve.wait_ge(y_done, pn + FREE)
                    b = S[2][:, :].rearrange("p (c n) -> p c n", c=2)
                    nc.vector.tensor_tensor(pq[:, 0:2, :], b, co, ALU.mult)
                    nc.vector.tensor_tensor(pq[:, 2:4, :], b, si, ALU.mult).then_inc(pq_done, 1)
                elif st == 1:
                    dve.wait_ge(r_done, pn + 1)
                    mag = sm[:, 4, bass.ds(pi, 1)].to_broadcast([P, SEQ])
                    for c in range(2):
                        nc.vector.tensor_tensor_scan(rr[:, c, :], mag, pq[:, c, :], 0.0, ALU.mult, ALU.add)
                    dve.drain()
                elif st == 2:
                    nc.vector.tensor_tensor(pq[:, 0:2, :], rr[:, :, :], co, ALU.mult)
                    nc.vector.tensor_tensor(pq[:, 2:4, :], rr[:, :, :], si, ALU.mult)
                    dve.drain()
                    nc.vector.tensor_tensor(pq[:, 0, :], pq[:, 0, :], pq[:, 3, :], ALU.subtract)
                    nc.vector.tensor_tensor(pq[:, 1, :], pq[:, 1, :], pq[:, 2, :], ALU.add).then_inc(xx_done, 1)

            for x_ in (*lo_ready, bias_used, xx_done, pq_done):
                dve.sem_inc(x_, FREE)
            dve.wait_ge(x_arrived, 16 * TT)
            for n in range(NSL):
                statistics(n)
            layer_norm(0, 0)
            for j in range(AHEAD):
                split_lo(0, j)
            with dve.Fori(0, DEPTH) as li:
                turn = li * lay
                for r in range(8):
                    tr = turn + 2 * r
                    for j in range(CPS):
                        split_lo(tr, j + AHEAD)
                        if r == 2 and j == 4:
                            dve.wait_ge(p_hi, li + 1)
                            for g in range(CT):
                                i_ = nc.vector.scalar_tensor_tensor(
                                    out=yT[1][:, 8 + g, :], in0=S[2 + g // 2][:, (g % 2) * SEQ:(g % 2 + 1) * SEQ],
                                    scalar=cp[:, PC_PSC + g:PC_PSC + g + 1], in1=yT[0][:, 8 + g, :].bitcast(F32),
                                    op0=ALU.mult, op1=ALU.subtract)
                            i_.then_inc(p_lo, 1)
                    if 2 <= r < 6:
                        dve.wait_ge(acc_free[r % 2], li * G_LAYER[r % 2] + (r // 2 + 1) + FREE)
                        s4 = stg[:, r % 2].rearrange("p t (g d) -> p t g d", d=QK)
                        x1, x2 = s4[:, :, :, 0:8], s4[:, :, :, 8:16]
                        cs = [rope[:, k].unsqueeze(2).to_broadcast([P, TT, 8, 8]) for k in range(2)]
                        nc.vector.tensor_tensor(rt[:, 0], x1, cs[0], ALU.mult)
                        nc.vector.tensor_tensor(rt[:, 1], x2, cs[1], ALU.mult)
                        nc.vector.tensor_tensor(rt[:, 2], x2, cs[0], ALU.mult)
                        nc.vector.tensor_tensor(rt[:, 3], x1, cs[1], ALU.mult)
                        dve.drain()
                        nc.vector.tensor_tensor(x1, rt[:, 0], rt[:, 1], ALU.subtract)
                        nc.vector.tensor_tensor(x2, rt[:, 2], rt[:, 3], ALU.add).then_inc(rope_done, 1)
                        dve.drain()
                with dve.Fori(0, CT) as i:
                    tg = turn + C_GATE // RING + i * 6
                    for j in range(3 * CPS):
                        split_lo(tg, j + AHEAD)
                        for hh in range(2):
                            if 0 <= j - 12 * hh <= 6:
                                head_step(j - 12 * hh, li * HEADS + i * 2 + hh, i * 2 + hh)
                        if 9 <= j < 21:
                            pp, st = divmod(j - 9, 3)
                            pair_step(st, li * PAIRS + i * PPT + pp, i * PPT + pp, pp, li * CT + i)
                        if j == 22:
                            dve.wait_ge(y_done, li * PAIRS + i * PPT + PPT + FREE)
                            ui = uT[:, bass.ds(i, 1), :].rearrange("p a n -> p (a n)")
                            nc.vector.scalar_tensor_tensor(out=gl[:, 0, :], in0=gl[:, 0, :], scalar=cp[:, bass.ds(i + PC_D, 1)],
                                                           in1=S[3][:, 0:SEQ], op0=ALU.mult, op1=ALU.add)
                            dve.drain()
                            nc.vector.tensor_tensor(gl[:, 1, :], gl[:, 0, :], gl[:, 0, :], ALU.mult)
                            dve.drain()
                            nc.vector.tensor_scalar(gl[:, 1, :], gl[:, 1, :], 0.044715, 1.0, ALU.mult, ALU.add)
                            dve.drain()
                            nc.vector.tensor_tensor(gl[:, 1, :], gl[:, 1, :], gl[:, 0, :], ALU.mult).then_inc(gelu_in, 1)
                        if j == 23:
                            dve.wait_ge(gelu_tanh, li * CT + i + 1)
                            nc.vector.scalar_tensor_tensor(out=ui, in0=gl[:, 1, :], scalar=1.0, in1=gl[:, 0, :],
                                                           op0=ALU.add, op1=ALU.mult).then_inc(y2_done, 1)
                        if j % CPS == CPS - 1:
                            s = j // CPS
                            b = s % 2
                            finished(dve, tg, j)
                            dve.wait_ge(bias_arrived, (li * 12 + i * 3 + s + 1) * 16)
                            dve.wait_ge(stg_stored[b], (li * (8, 4)[b] + i * (2, 1)[b] + s // 2) * 16 + 16 * FREE)
                            nc.vector.tensor_tensor(stg[:, b], acc[b][:, :, :], biasb[:, :].unsqueeze(1)
                                                    .to_broadcast([P, TT, NS]), ALU.add).then_inc(acc_free[b], 1)
                            dve.drain()
                            nc.vector.tensor_copy(rc[:, 0, 0:1], biasb[:, 0:1]).then_inc(bias_used, 1)
                            dve.drain()
                for n in range(NSL):
                    tp = turn + C_PROJ // RING + 2 * n
                    for j in range(CPS):
                        split_lo(tp, j + AHEAD)
                        if n == 0 and j == 2:
                            dve.wait_ge(glu_tanh, li + 1)
                            e4 = ex[:, :, :, :].rearrange("p a b n -> p (a b n)")
                            nc.vector.scalar_tensor_tensor(out=e4, in0=e4, scalar=1.0,
                                                           in1=uT[:, :, :].rearrange("p k n -> p (k n)"),
                                                           op0=ALU.add, op1=ALU.mult).then_inc(glu_prod, 1)
                            dve.wait_ge(glu_hi, li + 1)
                            nc.vector.scalar_tensor_tensor(out=yT[1][:, 12:16, :].rearrange("p k n -> p (k n)"), in0=e4,
                                                           scalar=0.25, in1=yT[0][:, 12:16, :].rearrange("p k n -> p (k n)")
                                                           .bitcast(F32), op0=ALU.mult, op1=ALU.subtract).then_inc(glu_lo, 1)
                        if n > 0 and j == 2:
                            t_units(8 + li * U_LAYER + U_MERGE + 2 * (n - 1), aT, 4 * (n - 1), 0.5)
                        if j in (3, 5, 7):
                            br = (3, 5, 7).index(j)
                            q = 3 * n + br
                            finished(dve, tp, j)
                            dve.wait_ge(gate_arrived[q % 2], (li * 6 + q // 2 + 1) * 16)
                            t_in = stg[:, q % 2]
                            pr = acc[q % 2][:, :, :]
                            if br == 0:
                                if n > 0:
                                    dve.wait_ge(t_bank, 8 + li * U_LAYER + U_MERGE + 2 * n)
                                nc.vector.scalar_tensor_tensor(out=merged[:, :, :], in0=t_in, scalar=1.0, in1=pr,
                                                               op0=ALU.add, op1=ALU.mult).then_inc(acc_free[q % 2], 1)
                                dve.drain()
                                nc.vector.tensor_copy(rc[:, 0, 0:1], merged[:, 0, 0:1]).then_inc(merge_done, 1)
                                dve.drain()
                            else:
                                nc.vector.scalar_tensor_tensor(out=t_in, in0=t_in, scalar=1.0, in1=pr,
                                                               op0=ALU.add, op1=ALU.mult).then_inc(acc_free[q % 2], 1)
                                dve.drain()
                                i_ = nc.vector.tensor_tensor(merged[:, :, :], merged[:, :, :], t_in, ALU.add)
                                i_.then_inc(merge_done, 1)
                                dve.drain()
                                if br == 2:
                                    nc.vector.tensor_copy(rc[:, 0, 0:1], merged[:, 0, 0:1]).then_inc(t_src, 2)
                                    dve.drain()
                for n in range(NSL):
                    tw = turn + C_WOUT // RING + 2 * n
                    for j in range(CPS):
                        split_lo(tw, j + AHEAD)
                        if n == 0 and j == 2:
                            t_units(8 + li * U_LAYER + U_MERGE + 6, aT, 12, 0.5)
                    finished(dve, tw, CPS - 1)
                    hs = h[:, :, n * NS:(n + 1) * NS]
                    nc.vector.scalar_tensor_tensor(out=hs, in0=hs, scalar=ALPHA, in1=acc[n % 2][:, :, :], op0=ALU.mult,
                                                   op1=ALU.add).then_inc(acc_free[n % 2], 1)
                    dve.drain()
                    statistics(n)
                layer_norm(li * 2 + 1, 8 + li * U_LAYER + U_LN1)
                wait_alone(dve, h_scaled, li + 1 + FREE)
                with dve.Fori(0, FF_GROUPS) as g:
                    tm = turn + C_MLP // RING + g * 16
                    um = 8 + li * U_LAYER + U_MLP + g * 8
                    for n in range(NSL):
                        for j in range(CPS):
                            split_lo(tm + 2 * n, j + AHEAD)
                            if n > 0 and j == 2:
                                t_units(um + 2 * (n - 1), yT, 4 * (n - 1))
                    for n in range(NSL):
                        for j in range(CPS):
                            split_lo(tm + 8 + 2 * n, j + AHEAD)
                            if n == 0 and j == 2:
                                t_units(um + 6, yT, 12)
                        finished(dve, tm + 8 + 2 * n, CPS - 1)
                        hs = h[:, :, n * NS:(n + 1) * NS]
                        nc.vector.tensor_tensor(hs, hs, acc[n % 2][:, :, :], ALU.add).then_inc(acc_free[n % 2], 1)
                        dve.drain()
                        statistics(n)
                layer_norm(li * 2 + 2, 8 + li * U_LAYER + U_LN2)
            nc.vector.tensor_copy(rc[:, 0, 0:1], h[:, 0, 0:1]).then_inc(h_final, 1)

        @block.gpsimd
        def _(pool):
            g_ = nc.gpsimd

            def tt_(o, a, b, op):
                return g_.tensor_tensor(o, a, b, op)

            def ts_(o, a, s1, s2=None, op0=ALU.mult, op1=None):
                pool.drain()
                return g_.tensor_scalar(o, a, s1, s2, op0, op1) if op1 is not None else g_.tensor_scalar(o, a, s1, None, op0)

            def step(o, a, b, op):
                pool.drain()
                return g_.tensor_tensor(o, a, b, op)

            def half_angle(a, t1, t2, half, half90):
                ts_(t1, a, 1.0 / (2 * math.pi), MAGIC, ALU.mult, ALU.add)
                ts_(t1, t1, -MAGIC, None, ALU.add)
                for c in (PI2_1, PI2_2, PI2_3):
                    ts_(t2, t1, -c)
                    step(a, a, t2, ALU.add)
                ts_(a, a, 0.5)
                ts_(half, a, math.pi / 2 * (1 - 2e-7), -math.pi / 2 * (1 - 2e-7), ALU.min, ALU.max)
                return ts_(half90, half, math.pi / 2, 3.1415925, ALU.add, ALU.min)

            def rstd_of(o, var, w):
                ts_(o, var, LN_EPS, None, ALU.add)
                return step(o, o, halfc[:, 0, 0:w], ALU.pow)

            def norm_rstd(q):
                wait_alone(pool, ln_var, q + 1)
                rstd_of(rstd[:, :], mv[:, :, 1:2].rearrange("p a b -> p (a b)"), TT).then_inc(ln_rstd, 1)

            pool.sem_inc(h_scaled, FREE)
            pool.sem_inc(cf_done, FREE)
            g_.memset(halfc[:, 0, :], -0.5)
            g_.memset(halfc[:, 1, :], -1.0)
            g_.memset(halfc[:, 2, :], math.e)
            pool.wait_ge(cst_arrived, 32)
            pf = sm[:, 7, 0:TT]
            g_.tensor_copy(pf, posi[:, :])
            pool.drain()
            ang = sm[:, 8, :].rearrange("p (t n) -> p t n", t=TT)
            tt_(ang, pf.unsqueeze(2).to_broadcast([P, TT, 8]), cst[:, CC_FREQ:CC_N].unsqueeze(1).to_broadcast([P, TT, 8]), ALU.mult)
            half_angle(sm[:, 8, :], sm[:, 9, :], sm[:, 10, :], sm[:, 0, :], sm[:, 1, :]).then_inc(ang_done, 1)
            pool.wait_ge(sin_done, 1)
            rs, rcs = rope[:, 0].rearrange("p t n -> p (t n)"), rope[:, 1].rearrange("p t n -> p (t n)")

            def full_angle(co, si, s2, c2, t1):
                tt_(t1, s2, s2, ALU.mult)
                step(si, s2, c2, ALU.mult)
                ts_(si, si, 2.0)
                return ts_(co, t1, -2.0, 1.0, ALU.mult, ALU.add)

            full_angle(rs, rcs, rs, rcs, sm[:, 9, :])
            norm_rstd(0)
            with pool.Fori(0, DEPTH) as li:
                wait_alone(pool, cp_arrived, (li + 1) * 32)
                lv = cp[:, PC_LAM:PC_N]
                step(lamt[:, :], lv[:, 0:2 * QK], lv[:, 2 * QK:4 * QK], ALU.mult)
                l3 = lamt[:, :].rearrange("p (a n) -> p a n", a=2)
                w = QK // 2
                while w >= 1:
                    step(l3[:, :, 0:w], l3[:, :, 0:w], l3[:, :, w:2 * w], ALU.add)
                    w //= 2
                step(lam[:, 0:2], halfc[:, 2, 0:2], l3[:, :, 0:1].rearrange("p a n -> p (a n)"), ALU.pow)
                step(lam[:, 2:3], lam[:, 1:2], lam[:, 0:1], ALU.subtract)
                step(lam[:, 3:4], lam[:, 2:3], cp[:, PC_LAMC:PC_LAMC + 1], ALU.subtract)
                step(subg[:, :], cp[:, PC_SUBG:PC_SUBG + 1], cp[:, PC_LAMC + 1:PC_LAMC + 2], ALU.mult)
                ts_(glubh[:, :], cp[:, PC_GLUB:PC_GLUB + CT], 0.5)
                ar, ai, ldt = (cp[:, c:c + PAIRS] for c in (PC_AR, PC_AI, PC_LDT))
                dt, mag = sm[:, 5, :], sm[:, 4, :]
                step(dt, halfc[:, 2, :], ldt, ALU.pow)
                step(sm[:, 6, :], ar, dt, ALU.mult)
                step(mag, halfc[:, 2, :], sm[:, 6, :], ALU.pow)
                step(sm[:, 8, :], ai, dt, ALU.mult)
                half_angle(sm[:, 8, :], sm[:, 9, :], sm[:, 10, :], sm[:, 0, :], sm[:, 1, :]).then_inc(ang_done, 1)
                wait_alone(pool, sin_done, li + 2)
                co, si = pw[:, 0, 0, :], pw[:, 0, 1, :]
                full_angle(co, si, sm[:, 2, :], sm[:, 3, :], sm[:, 9, :])
                nr, ni = sm[:, 6, :], sm[:, 7, :]
                step(nr, mag, co, ALU.mult)
                ts_(nr, nr, -1.0, None, ALU.add)
                step(ni, mag, si, ALU.mult)
                den, t1, t2 = sm[:, 8, :], sm[:, 9, :], sm[:, 10, :]
                tt_(t1, ar, ar, ALU.mult)
                tt_(t2, ai, ai, ALU.mult)
                step(den, t1, t2, ALU.add)
                step(den, den, halfc[:, 1, :], ALU.pow)
                for o, a, b, op in ((ff[:, 0, :], nr, ni, ALU.add), (ff[:, 1, :], ni, nr, ALU.subtract)):
                    step(t1, a, ar, ALU.mult)
                    tt_(t2, b, ai, ALU.mult)
                    step(t1, t1, t2, op)
                    step(o, t1, den, ALU.mult)
                for k in range(8):
                    pr, pi_ = pw[:, k, 0, :], pw[:, k, 1, :]
                    if k:
                        cr, ci = pw[:, k - 1, 0, :], pw[:, k - 1, 1, :]
                        step(t1, cr, cr, ALU.mult)
                        tt_(t2, ci, ci, ALU.mult)
                        step(pr, t1, t2, ALU.subtract)
                        tt_(pi_, cr, ci, ALU.mult)
                        ts_(pi_, pi_, 2.0)
                    step(t1, pr, pr, ALU.mult)
                    tt_(t2, pi_, pi_, ALU.mult)
                    step(t1, t1, t2, ALU.add)
                    ts_(t1, t1, -0.5, 1.5, ALU.mult, ALU.add)
                    step(pr, pr, t1, ALU.mult)
                    last = tt_(pi_, pi_, t1, ALU.mult)
                last.then_inc(params_done, 1)
                with pool.Fori(0, CT) as i:
                    tn = li * CT + i
                    wait_alone(pool, bc_arrived, (tn + 1) * 16)
                    wait_alone(pool, y_done, tn * PPT + FREE)
                    pool.drain()
                    fr, fi = [ff[:, c, bass.ds(i * PPT, PPT)].unsqueeze(2).to_broadcast([P, PPT, 32]) for c in range(2)]
                    cre, cim = [bc[:, 2 + c, :].rearrange("p (k n) -> p k n", k=PPT) for c in range(2)]
                    o_re, o_im = [cf[:, c, :].rearrange("p (k n) -> p k n", k=PPT) for c in range(2)]
                    s1 = rtmp[:, :, 0:32]
                    tt_(o_re, cre, fr, ALU.mult)
                    tt_(s1, cim, fi, ALU.mult)
                    step(o_re, o_re, s1, ALU.subtract)
                    step(s1, cim, fr, ALU.mult)
                    tt_(o_im, cre, fi, ALU.mult)
                    step(o_im, o_im, s1, ALU.add)
                    ts_(o_im, o_im, -1.0).then_inc(cf_done, 1)
                    wait_alone(pool, xx_done, tn * PPT + FREE)
                    g_.memset(rot[:, 0, :, 0:1], 1.0)
                    g_.memset(rot[:, 1, :, 0:1], 0.0)
                    for k in range(8):
                        n = 1 << k
                        c0, s0 = rot[:, 0, :, 0:n], rot[:, 1, :, 0:n]
                        c1, s1 = rot[:, 0, :, n:2 * n], rot[:, 1, :, n:2 * n]
                        er, ei = [pw[:, k, c, bass.ds(i * PPT, PPT)].unsqueeze(2).to_broadcast([P, PPT, n]) for c in range(2)]
                        tm_ = rtmp[:, :, 0:n]
                        step(c1, c0, er, ALU.mult)
                        tt_(tm_, s0, ei, ALU.mult)
                        tt_(s1, s0, er, ALU.mult)
                        step(c1, c1, tm_, ALU.subtract)
                        step(tm_, c0, ei, ALU.mult)
                        last = step(s1, s1, tm_, ALU.add)
                    last.then_inc(tab_done, 1)

                    def head_rms(hn):
                        wait_alone(pool, ss_done, hn + 1)
                        ts_(rms[:, :], ss[:, :], 1.0 / P, LN_EPS, ALU.mult, ALU.add)
                        step(rms[:, :], rms[:, :], halfc[:, 0, 0:2], ALU.pow).then_inc(rms_done, 1)

                    def pair_sum(pn):
                        wait_alone(pool, pq_done, pn + 1 + FREE)
                        tt_(pq[:, 0, :], pq[:, 0, :], pq[:, 3, :], ALU.add)
                        tt_(pq[:, 1, :], pq[:, 1, :], pq[:, 2, :], ALU.subtract).then_inc(r_done, 1)

                    head_rms(li * HEADS + i * 2)
                    for pp in range(2):
                        pair_sum(li * PAIRS + i * PPT + pp)
                    pair_sum(li * PAIRS + i * PPT + 2)
                    head_rms(li * HEADS + i * 2 + 1)
                    pair_sum(li * PAIRS + i * PPT + 3)
                norm_rstd(li * 2 + 1)
                wait_alone(pool, t_bank, 8 + li * U_LAYER + U_LN1 + 8)
                for tt in range(TT):
                    last = g_.tensor_scalar(h[:, tt, :], h[:, tt, :], ALPHA, None, ALU.mult)
                last.then_inc(h_scaled, 1)
                norm_rstd(li * 2 + 2)

        @block.tensor
        def _(pe):
            def products(turn, j, lhs, kt0, a, first, last, need=None):
                t, s = slot(turn, j)
                if need is not None:
                    pe.wait_ge(t_lo, need)
                pe.wait_ge(lo_ready[s], t + 1 + FREE)
                for k in range(CK):
                    for tt in range(TT):
                        hi = lhs[0][:, kt0 + k, tt * P:(tt + 1) * P]
                        lo = lhs[1][:, kt0 + k, tt * P:(tt + 1) * P]
                        o = acc[a][:, tt, :]
                        nc.tensor.matmul(o, hi, whi[:, s, k], start=first and k == 0, stop=False)
                        nc.tensor.matmul(o, hi, wlo[:, s, k], start=False, stop=False)
                        i_ = nc.tensor.matmul(o, lo, whi[:, s, k], start=False, stop=last and k == CK - 1)
                i_.then_inc(chunk_used[s], 1)

            def t_unit(u, par, src):
                pe.wait_ge(t_src, u + 1)
                if not (type(u) is int and u < 2):
                    pe.wait_ge(t_lo, u - 1)
                for q in range(4):
                    i_ = nc.tensor.transpose(S[par][:, q * P:(q + 1) * P], src[:, q * P:(q + 1) * P], ident)
                i_.then_inc(t_bank, 1)

            def ln_units(u0):
                for q in range(NSL):
                    for tt in range(TT):
                        t_unit(u0 + 2 * q + tt, tt, h[:, tt, q * NS:(q + 1) * NS])

            def head_step(st, hn, hd):
                if st == 0:
                    pe.wait_ge(q_copied, hn + 1)
                    for qt in range(2):
                        w = (qt + 1) * P
                        for c in range(2):
                            r = slice(c * QK, (c + 1) * QK)
                            nc.tensor.matmul(S[c][:, qt * P:qt * P + w], qs[r, 0, qt * P:(qt + 1) * P],
                                             qs[r, 1, 0:w], start=True, stop=True)
                            i_ = nc.tensor.matmul(S[c][:, 2 * qt * P:(2 * qt + 1) * P], ident, mask, start=False,
                                                  stop=True, skip_group_check=True)
                    i_.then_inc(score_done, 1)
                elif st == 2:
                    pe.wait_ge(at_done, hn + 1)
                    for b in range(3):
                        i_ = nc.tensor.transpose(S[0][:, b * P:(b + 1) * P], ats[:, b * P:(b + 1) * P], ident)
                    i_.then_inc(atT_done, 1)
                elif st == 3:
                    pe.wait_ge(atT_copied, hn + 1)
                    nc.tensor.matmul(S[1][:, 0:P], atT[:, 0:P], v[:, 0, bass.ds(hd * P, P)], start=True, stop=True)
                    nc.tensor.matmul(S[1][:, P:2 * P], atT[:, P:2 * P], v[:, 0, bass.ds(hd * P, P)], start=True, stop=False)
                    nc.tensor.matmul(S[1][:, P:2 * P], atT[:, 2 * P:3 * P], v[:, 1, bass.ds(hd * P, P)], start=False,
                                     stop=True).then_inc(pv_done, 1)
                elif st == 5:
                    pe.wait_ge(o_done, hn + 1)
                    for qt in range(2):
                        i_ = nc.tensor.transpose(S[0][:, qt * P:(qt + 1) * P], osb[:, qt, :], ident)
                    i_.then_inc(oT_done, 1)

            def pair_step(st, pn, i, pp, tn):
                r = slice(32 * pp, 32 * (pp + 1))
                if st == 0:
                    if pp == 0:
                        pe.wait_ge(bc_arrived, (tn + 1) * 16)
                        pe.wait_ge(u_copied, tn + 1)
                    pe.wait_ge(pq_done, pn + FREE)
                    for c in range(2):
                        i_ = nc.tensor.matmul(S[2][:, c * SEQ:(c + 1) * SEQ], bc[r, c, :], gl[r, 0, :], start=True, stop=True)
                    i_.then_inc(bu_done, 1)
                else:
                    if pp == 0:
                        pe.wait_ge(cf_done, tn + 1 + FREE)
                    pe.wait_ge(xx_done, pn + 1 + FREE)
                    for c in range(2):
                        i_ = nc.tensor.matmul(S[3][r, 0:SEQ], cf[:, c, r], pq[:, c, :], start=(c == 0), stop=(c == 1))
                    i_.then_inc(y_done, 1)

            for x_ in (*chunk_used, bu_done, y_done):
                pe.sem_inc(x_, FREE)
            pe.wait_ge(cst_arrived, 32)
            ln_units(0)
            with pe.Fori(0, DEPTH) as li:
                turn = li * lay
                u_in = li * U_LAYER + 8
                g0 = [li * G_LAYER[b] for b in range(2)]
                for r in range(8):
                    b = r % 2
                    pe.wait_ge(acc_free[b], g0[b] + r // 2 + FREE)
                    for j in range(CPS):
                        need = u_in - 8 + 2 * (j // 2) + 2 if r == 0 else None
                        products(turn + 2 * r, j, aT, CK * j, b, j == 0, j == CPS - 1, need)
                        if j == 1 and (r == 1 or 3 <= r <= 6):
                            xu = li * 10 + (0 if r == 1 else 2 * (r - 2))
                            pe.wait_ge(x_out, xu + FREE)
                            if r == 1:
                                pe.wait_ge(acc_free[0], g0[0] + 1 + FREE)
                            else:
                                pe.wait_ge(rope_done, li * 4 + r - 2)
                            for tt in range(TT):
                                for q in range(4):
                                    i_ = nc.tensor.transpose(S[2 + tt][:, q * P:(q + 1) * P],
                                                             stg[:, (r - 1) % 2, tt, q * P:(q + 1) * P], ident)
                                i_.then_inc(x_bank, 1)
                        if r == 2 and j == 1:
                            pe.wait_ge(acc_free[1], g0[1] + 1 + FREE)
                            pe.wait_ge(x_out, li * 10 + 2 + FREE)
                            for g in range(CT):
                                o = S[2 + g // 2][:, (g % 2) * SEQ:(g % 2 + 1) * SEQ]
                                cg = slice(g * P, (g + 1) * P)
                                nc.tensor.matmul(o[:, 0:P], stg[:, 1, 0, cg], mt[:, g, 0, :], start=True, stop=True)
                                nc.tensor.matmul(o[:, P:SEQ], stg[:, 1, 0, cg], mt[:, g, 1, :], start=True, stop=False)
                                i_ = nc.tensor.matmul(o[:, P:SEQ], stg[:, 1, 1, cg], mt[:, g, 2, :], start=False, stop=True)
                            i_.then_inc(p_mean, 1)
                        if r == 2 and j == 3:
                            pe.wait_ge(p_copy, li + 1)
                            pe.wait_ge(cp_arrived, (li + 1) * 32)
                            for g in range(CT):
                                i_ = nc.tensor.matmul(S[2 + g // 2][:, (g % 2) * SEQ:(g % 2 + 1) * SEQ], poolw[:, g, :],
                                                      pq[:, g, :], start=True, stop=True)
                            i_.then_inc(p_mix, 1)
                        if r == 3 and j == 0:
                            pe.wait_ge(p_lo, li + 1)
                with pe.Fori(0, CT) as i:
                    tg = turn + C_GATE // RING + i * 6
                    tn = li * CT + i
                    for j in range(3 * CPS):
                        s = j // CPS
                        b = s % 2
                        if j % CPS == 0:
                            pe.wait_ge(acc_free[b], g0[b] + i * (2, 1)[b] + (G_GATE[b] + s // 2) + FREE)
                        products(tg, j, aT, CK * (j % CPS), b, j % CPS == 0, j % CPS == CPS - 1)
                        for hh in range(2):
                            if 0 <= j - 12 * hh <= 5:
                                head_step(j - 12 * hh, li * HEADS + i * 2 + hh, i * 2 + hh)
                        if 8 <= j < 21 and (j - 8) % 3 == 0 and j < 20:
                            pp = (j - 8) // 3
                            pair_step(0, li * PAIRS + i * PPT + pp, i, pp, tn)
                        if 11 <= j < 21 and (j - 11) % 3 == 0:
                            pp = (j - 11) // 3
                            pair_step(1, li * PAIRS + i * PPT + pp, i, pp, tn)
                for n in range(NSL):
                    tp = turn + C_PROJ // RING + 2 * n
                    for j in range(CPS):
                        if j in (0, 4, 6):
                            q = 3 * n + (0, 4, 6).index(j)
                            pe.wait_ge(acc_free[q % 2], g0[q % 2] + (G_PROJ[q % 2] + q // 2) + FREE)
                        if n == 0 and j == 0:
                            pe.wait_ge(o_lo, (li + 1) * HEADS)
                        if n == 0 and j == 6:
                            pe.wait_ge(glu_lo, li + 1)
                        products(tp, j, yT, CK * j, q % 2, j in (0, 4, 6), j in (3, 5, 7))
                        if n == 0 and j < 2:
                            if j == 0:
                                pe.wait_ge(glu_arrived, (li + 1) * 16)
                                pe.wait_ge(y2_done, (li + 1) * CT)
                            for ot in (2 * j, 2 * j + 1):
                                for k in range(CT):
                                    i_ = nc.tensor.matmul(S[2 + j][:, (ot % 2) * SEQ:(ot % 2 + 1) * SEQ],
                                                          gluw[:, k, ot * P:(ot + 1) * P], uT[:, k, :], start=(k == 0),
                                                          stop=(k == CT - 1))
                            i_.then_inc(glu_mm, 1)
                        if n > 0 and j == 1:
                            for tt in range(TT):
                                t_unit(u_in + U_MERGE + 2 * (n - 1) + tt, tt, merged[:, tt, :])
                for n in range(NSL):
                    tw = turn + C_WOUT // RING + 2 * n
                    pe.wait_ge(acc_free[n % 2], g0[n % 2] + (G_WOUT[n % 2] + n // 2) + FREE)
                    for j in range(CPS):
                        need = u_in + U_MERGE + 2 * (j // 2) + 2 if n == 0 else None
                        products(tw, j, aT, CK * j, n % 2, j == 0, j == CPS - 1, need)
                        if n == 0 and j == 1:
                            for tt in range(TT):
                                t_unit(u_in + U_MERGE + 6 + tt, tt, merged[:, tt, :])
                ln_units(u_in + U_LN1)
                with pe.Fori(0, FF_GROUPS) as g:
                    tm = turn + C_MLP // RING + g * 16
                    um = u_in + U_MLP + g * 8
                    for n in range(2 * NSL):
                        up = n < NSL
                        pe.wait_ge(acc_free[n % 2], g0[n % 2] + g * 4 + (G_MLP[n % 2] + n // 2) + FREE)
                        for j in range(CPS):
                            need = None
                            if n == 0:
                                need = u_in + U_LN1 + 2 * (j // 2) + 2
                            if n == NSL:
                                need = um + 2 * (j // 2) + 2
                            products(tm + 2 * n, j, aT if up else yT, CK * j, n % 2, j == 0, j == CPS - 1, need)
                            if 0 < n <= NSL and j == 1:
                                for tt in range(TT):
                                    t_unit(um + 2 * (n - 1) + tt, tt, stg[:, (n - 1) % 2, tt, :])
                ln_units(u_in + U_LN2)


def _constants():
    c = np.zeros((P, CC_N), np.float32)
    c[:, CC_IDENT:CC_IDENT + P] = np.eye(P, dtype=np.float32)
    c[:, CC_MASK:CC_MASK + P] = np.where(np.arange(P)[None, :] > np.arange(P)[:, None], MASKED, 0.0)
    s, t = np.arange(SEQ)[:, None], np.arange(SEQ)[None, :]
    for g, w in enumerate(POOL_WINDOWS):
        m = ((s <= t) & (s > t - w)) / np.minimum(t + 1, w) - (s == t)
        for b, (a0, b0) in enumerate(((0, 0), (0, P), (P, P))):
            o = CC_MT + (g * 3 + b) * P
            c[:, o:o + P] = m[a0:a0 + P, b0:b0 + P]
    f = np.float32(ROPE_THETA) ** (-np.arange(0, ROT, 2, dtype=np.float32) / np.float32(ROT))
    c[:, CC_FREQ:CC_N] = f.astype(np.float32)
    return c


def _columns(a, lam):
    out = np.zeros((DEPTH, P, PC_N), np.float32)
    st = lambda z: z.reshape(DEPTH, PAIRS, P).transpose(0, 2, 1)
    out[:, :, PC_AR:PC_AR + PAIRS] = st(a["ssm_a_re"])
    out[:, :, PC_AI:PC_AI + PAIRS] = st(a["ssm_a_im"])
    out[:, :, PC_LDT:PC_LDT + PAIRS] = st(np.repeat(a["ssm_log_dt"][:, :, None], SSM_STATE, 2))
    for c, n in ((PC_D, "ssm_d"), (PC_GLUB, "glu_b"), (PC_PSC, "pool_scale")):
        out[:, :, c:c + CT] = a[n].reshape(DEPTH, CT, P).transpose(0, 2, 1)
    out[:, :, PC_SUBG] = a["subln_g"]
    out[:, :, PC_LAMC:PC_LAMC + 2] = lam[:, None, :]
    for k, n in enumerate(("lam_q1", "lam_q2", "lam_k1", "lam_k2")):
        out[:, :, PC_LAM + k * QK:PC_LAM + (k + 1) * QK] = a[n][:, None, :]
    return out


def _ssm_blocks(a):
    out = np.zeros((DEPTH, CT, P, 4, P), np.float32)
    for k, n in enumerate(("ssm_b_re", "ssm_b_im")):
        b = a[n].reshape(DEPTH, CT, PPT, 2, SSM_STATE, SSM_CH)
        for pp in range(PPT):
            for e in range(2):
                r = pp * 32 + e * SSM_CH
                out[:, :, r:r + SSM_CH, k, e * SSM_STATE:(e + 1) * SSM_STATE] = b[:, :, pp, e].transpose(0, 1, 3, 2)
    for k, n in enumerate(("ssm_c_re", "ssm_c_im")):
        c = a[n].reshape(DEPTH, CT, PPT, 2, SSM_CH, SSM_STATE)
        for pp in range(PPT):
            for e in range(2):
                r = pp * 32 + e * SSM_CH
                out[:, :, e * SSM_STATE:(e + 1) * SSM_STATE, 2 + k, r:r + SSM_CH] = c[:, :, pp, e].transpose(0, 1, 3, 2)
    return out


def kernel(**inputs):
    import concourse.bacc as bacc
    from concourse.bass_utils import run_bass_kernel_spmd

    a = {n: np.ascontiguousarray(z) for n, z in inputs.items()}
    init = [0.8 - 0.6 * math.exp(-0.3 * l) for l in range(DEPTH)]
    lam = np.array([[z, 1.0 - z] for z in init], np.float32)
    arrays = {
        "x": a["x"].reshape(SEQ, D_MODEL),
        "pos": np.ascontiguousarray(a["positions"].reshape(TT, P).T),
        "ln_in": np.stack([a["ln_in_g"], a["ln_in_b"]]),
        "w_in": a["w_in"], "b_gate": a["b_gate"],
        "colp": _columns(a, lam),
        "pool_w": a["pool_w"],
        "ssm_bc": _ssm_blocks(a),
        "glu_w": a["glu_w"], "proj_attn": a["proj_attn"], "proj_pool": a["proj_pool"], "proj_ssm": a["proj_ssm"],
        "w_out": a["w_out"],
        "ln1": np.stack([a["ln1_g"], a["ln1_b"]], 1),
        "w_up": a["w_up"], "w_down": a["w_down"],
        "ln2": np.stack([a["ln2_g"], a["ln2_b"]], 1),
        "consts": _constants(),
    }
    nc = bacc.Bacc("TRN2", target_bir_lowering=False, num_devices=1, dynamic_dma_scratch_size=1024)
    args = [nc.dram_tensor(f"{n}_dram", z.shape, mybir.dt.from_np(z.dtype), kind="ExternalInput").ap()
            for n, z in arrays.items()]
    gates = nc.dram_tensor("gates_dram", (TT, P, 3 * D_MODEL), mybir.dt.float32, kind="Internal").ap()
    out = nc.dram_tensor("out_dram", (SEQ, D_MODEL), mybir.dt.float32, kind="ExternalOutput").ap()
    build_trunk(nc, *args, gates, out)
    r = run_bass_kernel_spmd(nc, [{f"{n}_dram": z for n, z in arrays.items()}], core_ids=[0])
    return r.results[0]["out_dram"].reshape(1, SEQ, D_MODEL)
```

```python
import math

import numpy as np
import concourse.bass as bass
from concourse import mybir
from contextlib import ExitStack

D_MODEL = 2048
SEQ = 256
DEPTH = 2
HEADS = 8
QK = 64
ROT = QK // 4
ROPE_THETA = 500000.0
POOL_WINDOWS = (2, 4, 8, 16)
SSM_WIDTH = 512
SSM_CH = 16
SSM_STATE = 64
D_FF = 4 * D_MODEL
IN_COLS = 3 * HEADS * 2 * QK + 2 * SSM_WIDTH + 3 * D_MODEL
ALPHA = (2.0 * DEPTH) ** 0.25
LN_EPS = 1e-5

P = 128
TT = SEQ // P
NS = 512
KT = D_MODEL // P
CK = 2
CPS = KT // CK
RING = 4
AHEAD = 2
FREE = 1
FREE2 = 2
NSL = D_MODEL // NS
FF_GROUPS = D_FF // D_MODEL
GATE0 = IN_COLS - 3 * D_MODEL
POOL0 = 3 * HEADS * 2 * QK
SSM0 = POOL0 + SSM_WIDTH
PAIRS = SSM_WIDTH // (2 * SSM_CH)
PPT = P // (2 * SSM_CH)
CT = SSM_WIDTH // P

GS = 3 * NSL
TILE = GS // CT * CPS
HPT = HEADS // CT
HEAD_SHIFT = TILE // HPT
MERGES = 2 * NSL
X_UNITS = 5 * TT

C_WIN = 0
C_GATE = 8 * CPS
C_PROJ = C_GATE + GS * CPS
C_WOUT = C_PROJ + NSL * CPS
C_MLP = C_WOUT + NSL * CPS
C_LAYER = C_MLP + FF_GROUPS * 2 * NSL * CPS
G_GATE = 8
G_PROJ = G_GATE + GS
G_WOUT = G_PROJ + GS
G_MLP = G_WOUT + NSL
G_LAYER = G_MLP + FF_GROUPS * 2 * NSL
U_MERGE = 2 * NSL
U_LN1 = U_MERGE + 2 * NSL
U_MLP = U_LN1 + 2 * NSL
U_LAYER = U_MLP + 2 * NSL * FF_GROUPS
HEAD_PE = {1: "scores", 4: "transpose", 6: "values", 9: "out"}
HEAD_ACT = {0: "scores", 2: "exp", 5: "transpose", 7: "square", 10: "out"}
HEAD_DVE = {2: "max", 3: "combine", 8: "scale", 10: "out"}
GELU_IN, GELU_OUT = 21, 22
PAIR_BU, PAIR_Y = (3, 6, 10, 15), (7, 11, 16, 20)
PAIR_DVE = ((4, 5, 6), (7, 9, 10), (11, 12, 13), (16, 17, 18))

MASKED = -(2.0 ** 100)
MAGIC = 1.5 * 2.0 ** 23
PI2_1 = 6.28125
PI2_2 = 0.0019350051879882812
PI2_3 = 2 * math.pi - PI2_1 - PI2_2
GELU_C = math.sqrt(2.0 / math.pi)

PC_AR, PC_AI, PC_LDT = 0, PAIRS, 2 * PAIRS
PC_D = 3 * PAIRS
PC_GLUB = PC_D + CT
PC_PSC = PC_GLUB + CT
PC_SUBG = PC_PSC + CT
PC_LAMC = PC_SUBG + 1
PC_LAM = PC_LAMC + 2
PC_N = PC_LAM + 4 * QK
CC_IDENT = 0
CC_MASK = P
CC_FREQ = 2 * P
CC_MT = CC_FREQ + ROT // 2
CC_N = CC_MT + 12 * P


NORM_SPLITS = ((0,), (1, 2), (3, 4), (5, 6, 7))


def merges(q):
    return 2 * (q // 3) + q % 3


def build_trunk(nc, x, pos, ln_top, w_in, b_gate, colp, pool_w, ssm_bc, glu_w, proj_attn, proj_pool, proj_ssm,
                w_out, ln1, w_up, w_down, consts, gates_dram, out):
    F32, FR, I32 = mybir.dt.float32, mybir.dt.float32r, mybir.dt.int32
    ALU, ACT, AX = mybir.AluOpType, mybir.ActivationFunctionType, mybir.AxisListType
    ctx = ExitStack()
    with ctx:
        def sb(name, shape, dt=F32):
            return ctx.enter_context(nc.sbuf_tensor(name, shape, dt))

        def sem(name):
            return ctx.enter_context(nc.semaphore(name))

        raw = sb("raw", [P, RING, CK, NS])
        whi = sb("whi", [P, RING, CK, NS], FR)
        wlo = sb("wlo", [P, RING, CK, NS], FR)
        aT = [sb("aT_hi", [P, KT, SEQ], FR), sb("aT_lo", [P, KT, SEQ], FR)]
        yT = [sb("yT_hi", [P, KT, SEQ], FR), sb("yT_lo", [P, KT, SEQ], FR)]
        h = sb("h", [P, TT, D_MODEL])
        qk = sb("qk", [P, 2 * HEADS, SEQ])
        lnp = qk[:, :, :].rearrange("p a b -> p (a b)").rearrange("p (a n) -> p a n", a=2)
        v = sb("v", [P, TT, HEADS * P])
        gluw = v[:, :, :].rearrange("p a b -> p (a b)").rearrange("p (k n) -> p k n", k=CT)
        uT = sb("uT", [P, CT, SEQ])
        stg = sb("stg", [P, 2, TT, NS])
        merged = sb("merged", [P, TT, NS])
        rot = sb("rot", [P, 2, PPT, SEQ])
        rtmp = sb("rtmp", [P, 2, PPT, P])
        pq2 = sb("pq", [P, 2, 4, SEQ])
        pq = pq2[:, 0]
        rr = sb("rr", [P, 2, SEQ])
        gl = sb("gl", [P, 2, SEQ])
        ex = sb("ex", [P, 2, 2, SEQ])
        ats = sb("ats", [P, 3 * P])
        atT = sb("atT", [P, 3 * P])
        osb = sb("osb", [P, 2, P])
        junk = sb("junk", [P, P])
        qs = sb("qs", [P, 2, SEQ])
        bc = sb("bc", [P, 4, P])
        cf = sb("cf", [P, 2, P])
        poolw = sb("poolw", [P, CT, P])
        biasb = sb("biasb", [P, NS])
        cst = sb("cst", [P, CC_MT])
        ident = cst[:, CC_IDENT:CC_IDENT + P]
        mask = cst[:, CC_MASK:CC_MASK + P]
        mtl = v[:, :, :].rearrange("p a b -> p (a b)")[:, 0:12 * P]
        mt = mtl.rearrange("p (g b n) -> p g b n", g=4, b=3)
        identb = sb("identb", [P, P], mybir.dt.bfloat16)
        maskb = sb("maskb", [P, P], mybir.dt.bfloat16)
        cp = sb("cp", [P, PC_N])
        posi = sb("posi", [P, TT], I32)
        rope = sb("rope", [P, 2, TT, ROT // 2])
        rt = sb("rt", [P, 4, TT, 8, ROT // 2])
        sm = sb("sm", [P, 16, 16])
        pw = sb("pw", [P, 8, 2, 16])
        ff = sb("ff", [P, 2, 16])
        halfc = sb("halfc", [P, 4, 16])
        stats = sb("stats", [P, TT, NSL, 6])
        mv = sb("mv", [P, TT, 2])
        rstd = sb("rstd", [P, TT])
        mx = sb("mx", [P, 2, 2])
        sums = sb("sums", [P, 2, 2])
        rc = sb("rc", [P, 2, 2])
        ss = sb("ss", [P, 2])
        rms = sb("rms", [P, 2])
        lamt = sb("lamt", [P, 2 * QK])
        lam = sb("lam", [P, 4])
        subg = sb("subg", [P, 1])
        glubh = sb("glubh", [P, CT])

        acc = [ctx.enter_context(nc.psum_tensor(f"acc{i}", [P, TT, NS], F32)) for i in range(2)]
        S = [ctx.enter_context(nc.psum_tensor(f"side{i}", [P, NS], F32)) for i in range(4)]

        raw_arrived = [sem(f"raw_arrived{i}") for i in range(RING)]
        hi_ready = [sem(f"hi_ready{i}") for i in range(RING)]
        lo_ready = [sem(f"lo_ready{i}") for i in range(RING)]
        chunk_used = [sem(f"chunk_used{i}") for i in range(RING)]
        acc_free = [sem(f"acc_free{i}") for i in range(2)]
        half_done = sem("half_done")
        t_bank, t_hi, t_lo, hid_done = sem("t_bank"), sem("t_hi"), sem("t_lo"), sem("hid_done")
        x_bank, x_out, rope_done = sem("x_bank"), sem("x_out"), sem("rope_done")
        ln_var, ln_rstd, norm_out = sem("ln_var"), sem("ln_rstd"), sem("norm_out")
        lnp_arrived = [sem(f"lnp_arrived{i}") for i in range(NSL)]
        x_arrived = [sem(f"x_arrived{i}") for i in range(NSL)]
        cst_arrived, mt_arrived, cp_arrived = sem("cst_arrived"), sem("mt_arrived"), sem("cp_arrived")
        bc_arrived, glu_arrived, bias_arrived, out_stored = (sem("bc_arrived"), sem("glu_arrived"), sem("bias_arrived"),
                                                             sem("out_stored"))
        mask_ready = sem("mask_ready")
        stg_stored = [sem(f"stg_stored{i}") for i in range(2)]
        gate_arrived = [sem(f"gate_arrived{i}") for i in range(2)]
        gate_tanh, merge_done = sem("gate_tanh"), sem("merge_done")
        ang_done, sin_done, params_done = sem("ang_done"), sem("sin_done"), sem("params_done")
        p_mean, p_copy, p_mix, p_hi, p_lo = sem("p_mean"), sem("p_copy"), sem("p_mix"), sem("p_hi"), sem("p_lo")
        (q_copied, score_done, max_done, exp_done, at_done, atT_done, atT_copied, pv_done, ss_done, rms_done, o_done,
         oT_done, o_hi, o_lo) = [sem(n) for n in (
             "q_copied", "score_done", "max_done", "exp_done", "at_done", "atT_done", "atT_copied", "pv_done",
             "ss_done", "rms_done", "o_done", "oT_done", "o_hi", "o_lo")]
        u_copied, bu_done, pq_done, r_done, xx_done = (sem("u_copied"), sem("bu_done"), sem("pq_done"), sem("r_done"),
                                                       sem("xx_done"))
        tab_done, cf_done, y_done, gelu_in, gelu_tanh, y2_done = (sem("tab_done"), sem("cf_done"), sem("y_done"),
                                                                  sem("gelu_in"), sem("gelu_tanh"), sem("y2_done"))
        glu_mm, glu_tanh, glu_prod, glu_hi, glu_lo = (sem("glu_mm"), sem("glu_tanh"), sem("glu_prod"),
                                                      sem("glu_hi"), sem("glu_lo"))

        def slot(turn, j):
            return turn + j // RING, j % RING

        def finished(eng, turn, j):
            t, s = slot(turn, j)
            eng.wait_ge(chunk_used[s], t + 1 + FREE)

        def wait_alone(eng, what, value):
            value = value if isinstance(value, int) else eng.to_reg(value)
            eng.wait_ge(cst_arrived, 32)
            eng.wait_ge(what, value)

        def taken(pair, k):
            return acc_free[k % 2], pair + (k // 2 + 1 + FREE)

        lay = C_LAYER // RING
        layp = G_LAYER // 2
        block = ctx.enter_context(nc.Block())

        @block.sync
        def _(sp):
            def load(turn, j, w, li, k0, n0):
                t, s = slot(turn, j)
                wait_alone(sp, lo_ready[s], t + FREE)
                src = w[bass.ds(li, 1), bass.ds(k0, CK * P), bass.ds(n0, NS)]
                sp.dma_start(raw[:, s], src.rearrange("o (t p) n -> p (o t) n", p=P)).then_inc(raw_arrived[s], 16)

            def load_norm(gain_bias, li, slices=range(NSL)):
                for q in slices:
                    src = gain_bias[bass.ds(li, 1), :, q * NS:(q + 1) * NS]
                    sp.dma_start(lnp[:, :, q * NS:(q + 1) * NS], src.to_broadcast([P, 2, NS]))\
                        .then_inc(lnp_arrived[q], 16)

            def load_x(q):
                sp.dma_start(h[:, :, q * NS:(q + 1) * NS],
                             x[:, q * NS:(q + 1) * NS].rearrange("(t p) n -> p t n", p=P)).then_inc(x_arrived[q], 16)

            sp.dma_start(cst[:, 0:CC_MT], consts[:, 0:CC_MT]).then_inc(cst_arrived, 16)
            sp.dma_start(posi[:, :], pos).then_inc(cst_arrived, 16)
            for q in range(NSL):
                load_x(q)
            with sp.Fori(0, DEPTH) as li:
                turn = li * lay
                pair = li * layp
                for r, n0 in enumerate((SSM0, POOL0, 0, NS, 2 * NS, 3 * NS, 4 * NS, 5 * NS)):
                    for j in range(CPS):
                        load(turn + r * 2, j, w_in, li, j * CK * P, n0)
                        if r == 0 and j == 0:
                            wait_alone(sp, norm_out, li * (4 * NSL) + FREE)
                        if r == 0 and j == AHEAD - 1:
                            load_norm(ln_top, li)
                        if r == 0 and j == AHEAD:
                            sp.dma_start(cp[:, :], colp[bass.ds(li, 1)].rearrange("o p n -> (o p) n"))\
                                .then_inc(cp_arrived, 16)
                            sp.dma_start(poolw[:, :, :], pool_w[bass.ds(li, 1)].rearrange("o g c d -> c (o g) d"))\
                                .then_inc(cp_arrived, 16)
                            sp.dma_start(mtl, consts[:, CC_MT:CC_N]).then_inc(mt_arrived, 16)
                with sp.Fori(0, CT // 2) as ii:
                    for k in range(6):
                        i, s = ii * 2 + k // 3, k % 3
                        for j in range(CPS):
                            if s == 0 and j == 0:
                                wait_alone(sp, bu_done, li * PAIRS + i * PPT + FREE)
                                wait_alone(sp, cf_done, li * CT + i + FREE)
                                sp.dma_start(bc[:, :, :], ssm_bc[bass.ds(li, 1), bass.ds(i, 1)]
                                             .rearrange("o u p a n -> p (o u a) n")).then_inc(bc_arrived, 16)
                            load(turn + C_GATE // RING + ii * 12, k * CPS + j, w_in, li, j * CK * P,
                                 GATE0 + ii * (6 * NS) + k * NS)
                            if j == 6:
                                wait_alone(sp, *taken(pair + ii * 3, G_GATE + k - 1))
                                sp.dma_start(biasb[:, :], b_gate[bass.ds(li, 1), bass.ds(ii * (6 * NS) + k * NS, NS)]
                                             .to_broadcast([P, NS])).then_inc(bias_arrived, 16)
                for n in range(NSL):
                    for j in range(CPS):
                        w, k0 = ((proj_attn, j * CK * P) if j < 4 else
                                 (proj_pool, (j - 4) * CK * P) if j < 6 else (proj_ssm, (j - 6) * CK * P))
                        load(turn + C_PROJ // RING + n * 2, j, w, li, k0, n * NS)
                        if n == 0 and j == 0:
                            wait_alone(sp, pv_done, (li + 1) * HEADS)
                            sp.dma_start(gluw, glu_w[bass.ds(li, 1)].rearrange("o (k p) n -> p (o k) n", p=P))\
                                .then_inc(glu_arrived, 16)
                        if n == 2 and j == 0:
                            wait_alone(sp, score_done, (li + 1) * HEADS)
                            load_norm(ln1, li)
                for n in range(NSL):
                    for j in range(CPS):
                        load(turn + C_WOUT // RING + n * 2, j, w_out, li, j * CK * P, n * NS)
                with sp.Fori(0, FF_GROUPS) as g:
                    for n in range(NSL):
                        for j in range(CPS):
                            load(turn + C_MLP // RING + g * 16 + n * 2, j, w_up, li, j * CK * P, g * D_MODEL + n * NS)
                    for n in range(NSL):
                        for j in range(CPS):
                            load(turn + C_MLP // RING + g * 16 + 8 + n * 2, j, w_down, li,
                                 g * D_MODEL + j * CK * P, n * NS)
            for j in range(AHEAD):
                load(DEPTH * lay, j, w_in, 0, j * CK * P, SSM0)
            sp.wait_ge(norm_out, DEPTH * 4 * NSL + FREE)
            load_norm(ln_top, DEPTH)
            for q in range(NSL):
                for t in range(TT):
                    c = slice(q * NS, (q + 1) * NS)
                    sp.wait_ge(norm_out, 2 * DEPTH * NSL * TT + q * TT + t + 1 + FREE)
                    sp.dma_start(out[t * P:(t + 1) * P, c], h[:, t, c]).then_inc(out_stored, 16)
            sp.wait_ge(out_stored, 16 * NSL * TT)

        @block.scalar
        def _(act):
            def split_hi(turn, j):
                t, s = slot(turn, j)
                act.wait_ge(raw_arrived[s], (t + 1) * 16)
                act.wait_ge(chunk_used[s], t + FREE)
                nc.scalar.activation(whi[:, s], raw[:, s], ACT.Copy).then_inc(hi_ready[s], 1)

            def t_unit(u, par, dst, kt0, tt, scale=1.0):
                act.wait_ge(t_bank, u + 1)
                nc.scalar.activation(dst[0][:, kt0:kt0 + 4, tt * P:(tt + 1) * P],
                                     S[par][:, :].rearrange("p (k n) -> p k n", k=4), ACT.Copy, scale=scale)\
                    .then_inc(t_hi, 1)

            def t_units(u0, dst, kt0, scale=1.0):
                for tt in range(TT):
                    t_unit(u0 + tt, tt, dst, kt0, tt, scale)

            def norm_and_split(u0, turn):
                for q in range(NSL):
                    t_units(u0 + 2 * q, aT, 4 * q)
                    for j in NORM_SPLITS[q]:
                        split_hi(turn, j + AHEAD)

            def head_step(st, hn, hd):
                if st == "scores":
                    nc.scalar.activation(qs[:, :, :], qk[:, :, :].rearrange("p (a h) n -> p a h n", a=2)[:, :, bass.ds(hd, 1), :]
                                         .rearrange("p a h n -> p a (h n)"), ACT.Copy)\
                        .then_inc(q_copied, 1)
                elif st == "exp":
                    act.wait_ge(max_done, hn + 1)
                    for qt in range(2):
                        for c in range(2):
                            w = (qt + 1) * P
                            i_ = nc.scalar.activation(ex[:, qt, c, 0:w], S[c][:, qt * P:qt * P + w], ACT.Exp,
                                                      scale=QK ** -0.5, bias=mx[:, qt, c:c + 1],
                                                      accum_out=sums[:, qt, c:c + 1])
                    i_.then_inc(exp_done, 1)
                elif st == "transpose":
                    act.wait_ge(atT_done, hn + 1)
                    nc.scalar.activation(atT[:, :], S[0][:, 0:3 * P], ACT.Copy).then_inc(atT_copied, 1)
                elif st == "square":
                    act.wait_ge(pv_done, hn + 1)
                    for qt in range(2):
                        if qt:
                            act.drain()
                        i_ = nc.scalar.activation(junk[:, :], S[1][:, qt * P:(qt + 1) * P], ACT.Square,
                                                  accum_out=ss[:, qt:qt + 1])
                    i_.then_inc(ss_done, 1)
                elif st == "out":
                    act.wait_ge(oT_done, hn + 1)
                    nc.scalar.activation(yT[0][:, bass.ds(hd, 1), :].rearrange("p a n -> p (a n)"), S[0][:, 0:SEQ],
                                         ACT.Copy, scale=subg[:, 0:1]).then_inc(o_hi, 1)

            for x_ in (acc_free[0], acc_free[1], x_out):
                act.sem_inc(x_, FREE)
            for x_ in stg_stored:
                act.sem_inc(x_, 16 * FREE)
            act.wait_ge(ang_done, 1)
            for k in range(2):
                i_ = nc.scalar.activation(rope[:, k].rearrange("p t n -> p (t n)"), sm[:, k, :], ACT.Sin)
            i_.then_inc(sin_done, 1)
            for j in range(AHEAD):
                split_hi(0, j)
            with act.Fori(0, DEPTH) as li:
                turn = li * lay
                pair = li * layp
                u_in = li * U_LAYER
                for r in range(8):
                    tr = turn + 2 * r
                    if r == 0:
                        norm_and_split(u_in, tr)
                    for j in range(CPS):
                        if r > 0:
                            split_hi(tr, j + AHEAD)
                        if j == 2 and (r == 1 or 3 <= r <= 6):
                            xu = li * X_UNITS + (0 if r == 1 else 2 * (r - 2))
                            for tt in range(TT):
                                act.wait_ge(x_bank, xu + tt + 1)
                                dst = uT if r == 1 else qk
                                k0 = 0 if r == 1 else 4 * (r - 3)
                                nc.scalar.activation(dst[:, k0:k0 + 4, tt * P:(tt + 1) * P],
                                                     S[2 + tt][:, :].rearrange("p (k n) -> p k n", k=4), ACT.Copy)\
                                    .then_inc(x_out, 1)
                        if r == 2 and j == 2:
                            act.wait_ge(p_mean, li + 1)
                            for b in range(2):
                                i_ = nc.scalar.activation(pq[:, 2 * b:2 * b + 2, :],
                                                          S[2 + b][:, :].rearrange("p (g n) -> p g n", g=2), ACT.Copy)
                            i_.then_inc(p_copy, 1)
                        if r == 2 and j == 4:
                            act.wait_ge(p_mix, li + 1)
                            for g in range(CT):
                                i_ = nc.scalar.activation(yT[0][:, 8 + g, :], S[2 + g // 2][:, (g % 2) * SEQ:(g % 2 + 1) * SEQ],
                                                          ACT.Copy, scale=cp[:, PC_PSC + g:PC_PSC + g + 1])
                            i_.then_inc(p_hi, 1)
                        if r == 4 and j == 5:
                            act.wait_ge(ang_done, li + 2)
                            for k in range(2):
                                i_ = nc.scalar.activation(sm[:, 2 + k, :], sm[:, k, :], ACT.Sin)
                            i_.then_inc(sin_done, 1)
                    finished(act, tr, CPS - 1)
                    if r < 6:
                        nc.scalar.activation(stg[:, r % 2], acc[r % 2][:, :, :], ACT.Copy).then_inc(acc_free[r % 2], 1)
                    else:
                        nc.scalar.activation(v[:, :, (r - 6) * NS:(r - 5) * NS], acc[r % 2][:, :, :], ACT.Copy)\
                            .then_inc(acc_free[r % 2], 1)

                def gate_out(ii, k):
                    b = k % 2
                    act.wait_ge(*taken(pair + ii * 3, G_GATE + k))
                    nc.scalar.activation(stg[:, b], stg[:, b], ACT.Tanh, scale=0.5).then_inc(gate_tanh, 1)
                    act.wait_ge(gate_tanh, li * GS + ii * 6 + k + 1)
                    act.dma_start(gates_dram[:, :, bass.ds(ii * (6 * NS) + k * NS, NS)].rearrange("t p n -> p t n"),
                                  stg[:, b]).then_inc(stg_stored[b], 16)

                with act.Fori(0, CT // 2) as ii:
                    tg = turn + C_GATE // RING + ii * 12
                    for jj in range(6 * CPS):
                        i, j = ii * 2 + jj // TILE, jj % TILE
                        split_hi(tg, jj + AHEAD)
                        for hh in range(HPT):
                            if j - HEAD_SHIFT * hh in HEAD_ACT:
                                head_step(HEAD_ACT[j - HEAD_SHIFT * hh], li * HEADS + i * HPT + hh, i * HPT + hh)
                        if j == 1:
                            act.wait_ge(y2_done, li * CT + i + FREE)
                            nc.scalar.activation(gl[:, 0, :], uT[:, bass.ds(i, 1), :].rearrange("p a n -> p (a n)"),
                                                 ACT.Copy).then_inc(u_copied, 1)
                        if j == GELU_IN:
                            act.wait_ge(gelu_in, li * CT + i + 1)
                            nc.scalar.activation(gl[:, 1, :], gl[:, 1, :], ACT.Tanh, scale=GELU_C).then_inc(gelu_tanh, 1)
                        if jj > CPS and jj % CPS == 1:
                            gate_out(ii, jj // CPS - 1)
                    gate_out(ii, 5)
                for n in range(NSL):
                    tp = turn + C_PROJ // RING + 2 * n
                    for j in range(CPS):
                        split_hi(tp, j + AHEAD)
                        if j in (0, 4, 6):
                            br = (0, 4, 6).index(j)
                            q = 3 * n + br
                            if q < 2:
                                for b in range(2):
                                    act.wait_ge(stg_stored[b], (li + 1) * (16 * GS // 2) + 16 * FREE)
                            elif (q - 2) % 3 == 0:
                                act.wait_ge(*taken(pair, G_PROJ + q - 2))
                            else:
                                act.wait_ge(merge_done, li * MERGES + merges(q - 2))
                            act.dma_start(stg[:, q % 2], gates_dram[:, :, br * D_MODEL + n * NS:br * D_MODEL + (n + 1) * NS]
                                          .rearrange("t p n -> p t n")).then_inc(gate_arrived[q % 2], 16)
                        if n == 0 and j == 1:
                            for ot in range(CT):
                                act.wait_ge(glu_mm, li * 2 + ot // 2 + 1)
                                i_ = nc.scalar.activation(ex[:, ot // 2, ot % 2, :], S[2 + ot // 2][:, (ot % 2) * SEQ:(ot % 2 + 1) * SEQ],
                                                          ACT.Tanh, scale=0.25, bias=glubh[:, ot:ot + 1])
                            i_.then_inc(glu_tanh, 1)
                        if n == 0 and j == 2:
                            act.wait_ge(glu_prod, li + 1)
                            nc.scalar.activation(yT[0][:, 12:16, :], ex[:, :, :, :].rearrange("p a b n -> p (a b) n"),
                                                 ACT.Copy, scale=0.25).then_inc(glu_hi, 1)
                        if n > 0 and j == 2:
                            t_units(u_in + U_MERGE + 2 * (n - 1), aT, 4 * (n - 1), 0.5)
                for n in range(NSL):
                    tw = turn + C_WOUT // RING + 2 * n
                    for j in range(CPS):
                        split_hi(tw, j + AHEAD)
                        if n == 0 and j == 2:
                            t_units(u_in + U_MERGE + 6, aT, 12, 0.5)

                def hidden_group(g, first):
                    tm = turn + C_MLP // RING + g * 16
                    um = u_in + U_MLP + g * 8
                    for n in range(NSL):
                        if n == 0 and first:
                            norm_and_split(u_in + U_LN1, tm)
                        else:
                            for j in range(CPS):
                                split_hi(tm + 2 * n, j + AHEAD)
                                if n > 0 and j == 2:
                                    t_units(um + 2 * (n - 1), yT, 4 * (n - 1))
                        finished(act, tm + 2 * n, CPS - 1)
                        nc.scalar.activation(stg[:, n % 2], acc[n % 2][:, :, :], ACT.Relu).then_inc(acc_free[n % 2], 1)
                        act.drain()
                        nc.scalar.activation(stg[:, n % 2], stg[:, n % 2], ACT.Square).then_inc(hid_done, 1)
                    for n in range(NSL):
                        for j in range(CPS):
                            split_hi(tm + 8 + 2 * n, j + AHEAD)
                            if n == 0 and j == 2:
                                t_units(um + 6, yT, 12)

                hidden_group(0, True)
                with act.Fori(1, FF_GROUPS) as g:
                    hidden_group(g, False)

        @block.vector
        def _(dve):
            def split_lo(turn, j):
                t, s = slot(turn, j)
                dve.wait_ge(hi_ready[s], t + 1)
                nc.vector.tensor_tensor(wlo[:, s], raw[:, s], whi[:, s].bitcast(F32), ALU.subtract)\
                    .then_inc(lo_ready[s], 1)

            def t_unit(u, par, dst, kt0, tt, scale):
                dve.wait_ge(t_hi, u + 1)
                lo = dst[1][:, kt0:kt0 + 4, tt * P:(tt + 1) * P]
                hi = dst[0][:, kt0:kt0 + 4, tt * P:(tt + 1) * P].bitcast(F32)
                bank = S[par][:, :].rearrange("p (k n) -> p k n", k=4)
                if scale == 1.0:
                    nc.vector.tensor_tensor(lo, bank, hi, ALU.subtract).then_inc(t_lo, 1)
                else:
                    nc.vector.scalar_tensor_tensor(out=lo, in0=bank, scalar=scale, in1=hi, op0=ALU.mult,
                                                   op1=ALU.subtract).then_inc(t_lo, 1)

            def t_units(u0, dst, kt0, scale=1.0):
                for tt in range(TT):
                    t_unit(u0 + tt, tt, dst, kt0, tt, scale)

            def norm_variance(q):
                dve.drain()
                for tt in range(TT):
                    i_ = nc.vector.bn_aggr(mv[:, tt, :], stats[:, tt].rearrange("p a b -> p (a b)"))
                i_.then_inc(ln_var, 1)
                dve.drain()

            def norm_gain(q, n):
                c = slice(n * NS, (n + 1) * NS)
                wait_alone(dve, lnp_arrived[n], (q + 1) * 16)
                for tt in range(TT):
                    nc.vector.scalar_tensor_tensor(out=h[:, tt, c], in0=h[:, tt, c], scalar=mv[:, tt, 0:1],
                                                   in1=lnp[:, 0, c], op0=ALU.subtract, op1=ALU.mult)

            def norm_bias(q, n):
                c = slice(n * NS, (n + 1) * NS)
                if n == 0:
                    dve.wait_ge(ln_rstd, q + 1)
                for tt in range(TT):
                    nc.vector.scalar_tensor_tensor(out=h[:, tt, c], in0=h[:, tt, c], scalar=rstd[:, tt:tt + 1],
                                                   in1=lnp[:, 1, c], op0=ALU.mult, op1=ALU.add).then_inc(norm_out, 1)

            def norm_slice(q, n):
                norm_gain(q, n)
                dve.drain()
                norm_bias(q, n)

            def norm_and_split(q, u0, turn):
                norm_variance(q)
                norm_slice(q, 0)
                for n in range(NSL):
                    t_units(u0 + 2 * n, aT, 4 * n)
                    if n + 1 < NSL:
                        norm_slice(q, n + 1)
                    for j in NORM_SPLITS[n]:
                        split_lo(turn, j + AHEAD)

            def statistics(n, tt):
                nc.vector.bn_stats(stats[:, tt, n, :], h[:, tt, n * NS:(n + 1) * NS])

            def residual(group, a, turn, n, scaled):
                for tt in range(TT):
                    if tt == 0:
                        dve.wait_ge(half_done, group + 1)
                    else:
                        finished(dve, turn, CPS - 1)
                    hs = h[:, tt, n * NS:(n + 1) * NS]
                    if scaled:
                        i_ = nc.vector.tensor_tensor(hs, hs, acc[a][:, tt, :], ALU.add)
                    else:
                        i_ = nc.vector.scalar_tensor_tensor(out=hs, in0=hs, scalar=ALPHA, in1=acc[a][:, tt, :],
                                                            op0=ALU.mult, op1=ALU.add)
                    if tt == 1:
                        i_.then_inc(acc_free[a], 1)
                    dve.drain()
                    statistics(n, tt)

            def head_step(st, hn, hd):
                if st == "max":
                    dve.wait_ge(score_done, hn + 1)
                    for qt in range(2):
                        for c in range(2):
                            nc.vector.reduce_max(rc[:, qt, c:c + 1], S[c][:, qt * P:(2 * qt + 1) * P], AX.X)
                    dve.drain()
                    nc.vector.tensor_scalar(mx[:, :, :], rc[:, :, :], -(QK ** -0.5), None, ALU.mult)\
                        .then_inc(max_done, 1)
                elif st == "combine":
                    dve.wait_ge(exp_done, hn + 1)
                    nc.vector.reciprocal(rc[:, :, :], sums[:, :, :])
                    dve.drain()
                    nc.vector.tensor_scalar(mx[:, :, 1:2], rc[:, :, 1:2], lam[:, 3:4], None, ALU.mult)
                    dve.drain()
                    for qt in range(2):
                        nc.vector.tensor_scalar(ex[:, qt, 1, 0:(qt + 1) * P], ex[:, qt, 1, 0:(qt + 1) * P],
                                                mx[:, qt, 1:2], None, ALU.mult)
                    dve.drain()
                    for qt in range(2):
                        i_ = nc.vector.scalar_tensor_tensor(
                            out=ats[:, qt * P:(2 * qt + 1) * P], in0=ex[:, qt, 0, 0:(qt + 1) * P],
                            scalar=rc[:, qt, 0:1], in1=ex[:, qt, 1, 0:(qt + 1) * P], op0=ALU.mult, op1=ALU.add)
                    i_.then_inc(at_done, 1)
                elif st == "scale":
                    dve.wait_ge(rms_done, hn + 1)
                    for qt in range(2):
                        i_ = nc.vector.tensor_scalar(osb[:, qt, :], S[1][:, qt * P:(qt + 1) * P], rms[:, qt:qt + 1], None,
                                                     ALU.mult)
                    i_.then_inc(o_done, 1)
                elif st == "out":
                    dve.wait_ge(o_hi, hn + 1)
                    nc.vector.scalar_tensor_tensor(
                        out=yT[1][:, bass.ds(hd, 1), :].rearrange("p a n -> p (a n)"), in0=S[0][:, 0:SEQ],
                        scalar=subg[:, 0:1], in1=yT[0][:, bass.ds(hd, 1), :].rearrange("p a n -> p (a n)").bitcast(F32),
                        op0=ALU.mult, op1=ALU.subtract).then_inc(o_lo, 1)

            def pair_step(st, pn, pi, pp, tn):
                pq = pq2[:, pp % 2]
                co = rot[:, 0, pp, :].unsqueeze(1).to_broadcast([P, 2, SEQ])
                si = rot[:, 1, pp, :].unsqueeze(1).to_broadcast([P, 2, SEQ])
                if st == 0:
                    if pp == 0:
                        dve.wait_ge(tab_done, tn + 1)
                    dve.wait_ge(bu_done, pn + 1 + FREE)
                    dve.wait_ge(y_done, pn - 1 + FREE2)
                    b = S[2][:, :].rearrange("p (c n) -> p c n", c=2)
                    nc.vector.tensor_tensor(pq[:, 0:2, :], b, co, ALU.mult)
                    nc.vector.tensor_tensor(pq[:, 2:4, :], b, si, ALU.mult).then_inc(pq_done, 1)
                elif st == 1:
                    dve.wait_ge(r_done, pn + 1)
                    mag = sm[:, 4, bass.ds(pi, 1)].to_broadcast([P, SEQ])
                    for c in range(2):
                        nc.vector.tensor_tensor_scan(rr[:, c, :], mag, pq[:, c, :], 0.0, ALU.mult, ALU.add)
                    dve.drain()
                elif st == 2:
                    nc.vector.tensor_tensor(pq[:, 0:2, :], rr[:, :, :], co, ALU.mult)
                    nc.vector.tensor_tensor(pq[:, 2:4, :], rr[:, :, :], si, ALU.mult)
                    dve.drain()
                    nc.vector.tensor_tensor(pq[:, 0, :], pq[:, 0, :], pq[:, 3, :], ALU.subtract)
                    nc.vector.tensor_tensor(pq[:, 1, :], pq[:, 1, :], pq[:, 2, :], ALU.add).then_inc(xx_done, 1)

            for x_ in (*lo_ready, xx_done, pq_done, norm_out, y2_done, t_lo, t_lo):
                dve.sem_inc(x_, FREE)
            for n in range(NSL):
                dve.wait_ge(x_arrived[n], 16)
                for tt in range(TT):
                    statistics(n, tt)
            for j in range(AHEAD):
                split_lo(0, j)
            with dve.Fori(0, DEPTH) as li:
                turn = li * lay
                pair = li * layp
                u_in = li * U_LAYER
                for r in range(8):
                    tr = turn + 2 * r
                    if r == 0:
                        norm_and_split(li * 2, u_in, tr)
                    for j in range(CPS):
                        if r > 0:
                            split_lo(tr, j + AHEAD)
                        if r == 2 and j == 4:
                            dve.wait_ge(p_hi, li + 1)
                            for g in range(CT):
                                i_ = nc.vector.scalar_tensor_tensor(
                                    out=yT[1][:, 8 + g, :], in0=S[2 + g // 2][:, (g % 2) * SEQ:(g % 2 + 1) * SEQ],
                                    scalar=cp[:, PC_PSC + g:PC_PSC + g + 1], in1=yT[0][:, 8 + g, :].bitcast(F32),
                                    op0=ALU.mult, op1=ALU.subtract)
                            i_.then_inc(p_lo, 1)
                    if 2 <= r < 6:
                        dve.wait_ge(*taken(pair, r))
                        s4 = stg[:, r % 2].rearrange("p t (g d) -> p t g d", d=QK)
                        x1, x2 = s4[:, :, :, 0:8], s4[:, :, :, 8:16]
                        cs = [rope[:, k].unsqueeze(2).to_broadcast([P, TT, 8, 8]) for k in range(2)]
                        nc.vector.tensor_tensor(rt[:, 0], x1, cs[0], ALU.mult)
                        nc.vector.tensor_tensor(rt[:, 1], x2, cs[1], ALU.mult)
                        nc.vector.tensor_tensor(rt[:, 2], x2, cs[0], ALU.mult)
                        nc.vector.tensor_tensor(rt[:, 3], x1, cs[1], ALU.mult)
                        dve.drain()
                        nc.vector.tensor_tensor(x1, rt[:, 0], rt[:, 1], ALU.subtract)
                        nc.vector.tensor_tensor(x2, rt[:, 2], rt[:, 3], ALU.add).then_inc(rope_done, 1)
                        dve.drain()

                def gate_bias(ii, k):
                    b = k % 2
                    finished(dve, turn + C_GATE // RING + ii * 12, k * CPS + CPS - 1)
                    dve.wait_ge(bias_arrived, (li * GS + ii * 6 + k + 1) * 16)
                    dve.wait_ge(stg_stored[b], (li * 6 + ii * 3 + k // 2) * 16 + 16 * FREE)
                    nc.vector.tensor_tensor(stg[:, b], acc[b][:, :, :], biasb[:, :].unsqueeze(1)
                                            .to_broadcast([P, TT, NS]), ALU.add).then_inc(acc_free[b], 1)

                with dve.Fori(0, CT // 2) as ii:
                    tg = turn + C_GATE // RING + ii * 12
                    for jj in range(6 * CPS):
                        i, j = ii * 2 + jj // TILE, jj % TILE
                        split_lo(tg, jj + AHEAD)
                        for hh in range(HPT):
                            if j - HEAD_SHIFT * hh in HEAD_DVE:
                                head_step(HEAD_DVE[j - HEAD_SHIFT * hh], li * HEADS + i * HPT + hh, i * HPT + hh)
                        for pp in range(PPT):
                            if j in PAIR_DVE[pp]:
                                pair_step(PAIR_DVE[pp].index(j), li * PAIRS + i * PPT + pp, i * PPT + pp, pp, li * CT + i)
                        if j == GELU_IN:
                            dve.wait_ge(y_done, li * PAIRS + i * PPT + PPT + FREE2)
                            ui = uT[:, bass.ds(i, 1), :].rearrange("p a n -> p (a n)")
                            nc.vector.scalar_tensor_tensor(out=gl[:, 0, :], in0=gl[:, 0, :], scalar=cp[:, bass.ds(i + PC_D, 1)],
                                                           in1=S[3][:, 0:SEQ], op0=ALU.mult, op1=ALU.add)
                            dve.drain()
                            nc.vector.tensor_tensor(gl[:, 1, :], gl[:, 0, :], gl[:, 0, :], ALU.mult)
                            dve.drain()
                            nc.vector.tensor_scalar(gl[:, 1, :], gl[:, 1, :], 0.044715, 1.0, ALU.mult, ALU.add)
                            dve.drain()
                            nc.vector.tensor_tensor(gl[:, 1, :], gl[:, 1, :], gl[:, 0, :], ALU.mult).then_inc(gelu_in, 1)
                        if j == GELU_OUT:
                            dve.wait_ge(gelu_tanh, li * CT + i + 1)
                            nc.vector.scalar_tensor_tensor(out=ui, in0=gl[:, 1, :], scalar=1.0, in1=gl[:, 0, :],
                                                           op0=ALU.add, op1=ALU.mult).then_inc(y2_done, 1)
                        if jj >= CPS and jj % CPS == 0:
                            gate_bias(ii, jj // CPS - 1)
                    gate_bias(ii, 5)
                for n in range(NSL):
                    tp = turn + C_PROJ // RING + 2 * n
                    for j in range(CPS):
                        split_lo(tp, j + AHEAD)
                        if n == 0 and j == 2:
                            dve.wait_ge(glu_tanh, li + 1)
                            e4 = ex[:, :, :, :].rearrange("p a b n -> p (a b n)")
                            nc.vector.scalar_tensor_tensor(out=e4, in0=e4, scalar=1.0,
                                                           in1=uT[:, :, :].rearrange("p k n -> p (k n)"),
                                                           op0=ALU.add, op1=ALU.mult).then_inc(glu_prod, 1)
                            dve.wait_ge(glu_hi, li + 1)
                            nc.vector.scalar_tensor_tensor(out=yT[1][:, 12:16, :].rearrange("p k n -> p (k n)"), in0=e4,
                                                           scalar=0.25, in1=yT[0][:, 12:16, :].rearrange("p k n -> p (k n)")
                                                           .bitcast(F32), op0=ALU.mult, op1=ALU.subtract).then_inc(glu_lo, 1)
                        if n > 0 and j == 2:
                            t_units(u_in + U_MERGE + 2 * (n - 1), aT, 4 * (n - 1), 0.5)
                        if j in (3, 5, 7):
                            br = (3, 5, 7).index(j)
                            q = 3 * n + br
                            finished(dve, tp, j)
                            dve.wait_ge(gate_arrived[q % 2], (li * 6 + q // 2 + 1) * 16)
                            t_in = stg[:, q % 2]
                            pr = acc[q % 2][:, :, :]
                            if br == 0:
                                if n > 0:
                                    dve.wait_ge(t_bank, u_in + U_MERGE + 2 * n)
                                nc.vector.scalar_tensor_tensor(out=merged[:, :, :], in0=t_in, scalar=1.0, in1=pr,
                                                               op0=ALU.add, op1=ALU.mult).then_inc(acc_free[q % 2], 1)
                            else:
                                nc.vector.scalar_tensor_tensor(out=t_in, in0=t_in, scalar=1.0, in1=pr,
                                                               op0=ALU.add, op1=ALU.mult).then_inc(acc_free[q % 2], 1)
                                dve.drain()
                                nc.vector.tensor_tensor(merged[:, :, :], merged[:, :, :], t_in, ALU.add)\
                                    .then_inc(merge_done, 1)
                for n in range(NSL):
                    tw = turn + C_WOUT // RING + 2 * n
                    for j in range(CPS):
                        split_lo(tw, j + AHEAD)
                        if n == 0 and j == 2:
                            t_units(u_in + U_MERGE + 6, aT, 12, 0.5)
                    residual(li * G_LAYER + (G_WOUT + n), n % 2, tw, n, False)

                def hidden_group(g, first):
                    tm = turn + C_MLP // RING + g * 16
                    um = u_in + U_MLP + g * 8
                    for n in range(NSL):
                        if n == 0 and first:
                            norm_and_split(li * 2 + 1, u_in + U_LN1, tm)
                        else:
                            for j in range(CPS):
                                split_lo(tm + 2 * n, j + AHEAD)
                                if n > 0 and j == 2:
                                    t_units(um + 2 * (n - 1), yT, 4 * (n - 1))
                    for n in range(NSL):
                        group = li * G_LAYER + g * (2 * NSL) + (G_MLP + NSL + n)
                        for j in range(CPS):
                            split_lo(tm + 8 + 2 * n, j + AHEAD)
                            if n == 0 and j == 2:
                                t_units(um + 6, yT, 12)
                        residual(group, n % 2, tm + 8 + 2 * n, n, not first)

                hidden_group(0, True)
                with dve.Fori(1, FF_GROUPS) as g:
                    hidden_group(g, False)
            norm_variance(2 * DEPTH)
            for half in range(0, NSL, 2):
                for n in (half, half + 1):
                    norm_gain(2 * DEPTH, n)
                dve.drain()
                for n in (half, half + 1):
                    norm_bias(2 * DEPTH, n)

        @block.gpsimd
        def _(pool):
            g_ = nc.gpsimd

            def tt_(o, a, b, op):
                return g_.tensor_tensor(o, a, b, op)

            def ts_(o, a, s1, s2=None, op0=ALU.mult, op1=None):
                pool.drain()
                return g_.tensor_scalar(o, a, s1, s2, op0, op1) if op1 is not None else g_.tensor_scalar(o, a, s1, None, op0)

            def step(o, a, b, op):
                pool.drain()
                return g_.tensor_tensor(o, a, b, op)

            def half_angle(a, t1, t2, half, half90):
                ts_(t1, a, 1.0 / (2 * math.pi), MAGIC, ALU.mult, ALU.add)
                ts_(t1, t1, -MAGIC, None, ALU.add)
                for c in (PI2_1, PI2_2, PI2_3):
                    ts_(t2, t1, -c)
                    step(a, a, t2, ALU.add)
                ts_(a, a, 0.5)
                ts_(half, a, math.pi / 2 * (1 - 2e-7), -math.pi / 2 * (1 - 2e-7), ALU.min, ALU.max)
                return ts_(half90, half, math.pi / 2, 3.1415925, ALU.add, ALU.min)

            def rstd_of(o, var, w):
                ts_(o, var, LN_EPS, None, ALU.add)
                return step(o, o, halfc[:, 0, 0:w], ALU.pow)

            def norm_rstd(q):
                wait_alone(pool, ln_var, q + 1)
                rstd_of(rstd[:, :], mv[:, :, 1:2].rearrange("p a b -> p (a b)"), TT).then_inc(ln_rstd, 1)

            pool.sem_inc(cf_done, FREE)
            g_.memset(halfc[:, 0, :], -0.5)
            g_.memset(halfc[:, 1, :], -1.0)
            g_.memset(halfc[:, 2, :], math.e)
            pool.wait_ge(cst_arrived, 32)
            g_.tensor_copy(identb[:, :], ident)
            g_.tensor_copy(maskb[:, :], mask).then_inc(mask_ready, 1)
            pf = sm[:, 7, 0:TT]
            g_.tensor_copy(pf, posi[:, :])
            pool.drain()
            ang = sm[:, 8, :].rearrange("p (t n) -> p t n", t=TT)
            tt_(ang, pf.unsqueeze(2).to_broadcast([P, TT, 8]), cst[:, CC_FREQ:CC_MT].unsqueeze(1).to_broadcast([P, TT, 8]), ALU.mult)
            half_angle(sm[:, 8, :], sm[:, 9, :], sm[:, 10, :], sm[:, 0, :], sm[:, 1, :]).then_inc(ang_done, 1)
            pool.wait_ge(sin_done, 1)
            rs, rcs = rope[:, 0].rearrange("p t n -> p (t n)"), rope[:, 1].rearrange("p t n -> p (t n)")

            def full_angle(co, si, s2, c2, t1):
                tt_(t1, s2, s2, ALU.mult)
                step(si, s2, c2, ALU.mult)
                ts_(si, si, 2.0)
                return ts_(co, t1, -2.0, 1.0, ALU.mult, ALU.add)

            full_angle(rs, rcs, rs, rcs, sm[:, 9, :])
            with pool.Fori(0, DEPTH) as li:
                norm_rstd(li * 2)
                wait_alone(pool, cp_arrived, (li + 1) * 32)
                lv = cp[:, PC_LAM:PC_N]
                step(lamt[:, :], lv[:, 0:2 * QK], lv[:, 2 * QK:4 * QK], ALU.mult)
                l3 = lamt[:, :].rearrange("p (a n) -> p a n", a=2)
                w = QK // 2
                while w >= 1:
                    step(l3[:, :, 0:w], l3[:, :, 0:w], l3[:, :, w:2 * w], ALU.add)
                    w //= 2
                step(lam[:, 0:2], halfc[:, 2, 0:2], l3[:, :, 0:1].rearrange("p a n -> p (a n)"), ALU.pow)
                step(lam[:, 2:3], lam[:, 1:2], lam[:, 0:1], ALU.subtract)
                step(lam[:, 3:4], lam[:, 2:3], cp[:, PC_LAMC:PC_LAMC + 1], ALU.subtract)
                step(subg[:, :], cp[:, PC_SUBG:PC_SUBG + 1], cp[:, PC_LAMC + 1:PC_LAMC + 2], ALU.mult)
                ts_(glubh[:, :], cp[:, PC_GLUB:PC_GLUB + CT], 0.5)
                ar, ai, ldt = (cp[:, c:c + PAIRS] for c in (PC_AR, PC_AI, PC_LDT))
                dt, mag = sm[:, 5, :], sm[:, 4, :]
                step(dt, halfc[:, 2, :], ldt, ALU.pow)
                step(sm[:, 6, :], ar, dt, ALU.mult)
                step(mag, halfc[:, 2, :], sm[:, 6, :], ALU.pow)
                step(sm[:, 8, :], ai, dt, ALU.mult)
                half_angle(sm[:, 8, :], sm[:, 9, :], sm[:, 10, :], sm[:, 0, :], sm[:, 1, :]).then_inc(ang_done, 1)
                wait_alone(pool, sin_done, li + 2)
                co, si = pw[:, 0, 0, :], pw[:, 0, 1, :]
                full_angle(co, si, sm[:, 2, :], sm[:, 3, :], sm[:, 9, :])
                nr, ni = sm[:, 6, :], sm[:, 7, :]
                step(nr, mag, co, ALU.mult)
                ts_(nr, nr, -1.0, None, ALU.add)
                step(ni, mag, si, ALU.mult)
                den, t1, t2 = sm[:, 8, :], sm[:, 9, :], sm[:, 10, :]
                tt_(t1, ar, ar, ALU.mult)
                tt_(t2, ai, ai, ALU.mult)
                step(den, t1, t2, ALU.add)
                step(den, den, halfc[:, 1, :], ALU.pow)
                for o, a, b, op in ((ff[:, 0, :], nr, ni, ALU.add), (ff[:, 1, :], ni, nr, ALU.subtract)):
                    step(t1, a, ar, ALU.mult)
                    tt_(t2, b, ai, ALU.mult)
                    step(t1, t1, t2, op)
                    step(o, t1, den, ALU.mult)
                for k in range(8):
                    pr, pi_ = pw[:, k, 0, :], pw[:, k, 1, :]
                    if k:
                        cr, ci = pw[:, k - 1, 0, :], pw[:, k - 1, 1, :]
                        step(t1, cr, cr, ALU.mult)
                        tt_(t2, ci, ci, ALU.mult)
                        step(pr, t1, t2, ALU.subtract)
                        tt_(pi_, cr, ci, ALU.mult)
                        ts_(pi_, pi_, 2.0)
                    step(t1, pr, pr, ALU.mult)
                    tt_(t2, pi_, pi_, ALU.mult)
                    step(t1, t1, t2, ALU.add)
                    ts_(t1, t1, -0.5, 1.5, ALU.mult, ALU.add)
                    step(pr, pr, t1, ALU.mult)
                    last = tt_(pi_, pi_, t1, ALU.mult)
                last.then_inc(params_done, 1)
                with pool.Fori(0, CT) as i:
                    tn = li * CT + i
                    wait_alone(pool, xx_done, tn * PPT + FREE)
                    g_.memset(rot[:, 0, :, 0:1], 1.0)
                    g_.memset(rot[:, 1, :, 0:1], 0.0)
                    for k in range(8):
                        n = 1 << k
                        c0, s0 = rot[:, 0, :, 0:n], rot[:, 1, :, 0:n]
                        c1, s1 = rot[:, 0, :, n:2 * n], rot[:, 1, :, n:2 * n]
                        er, ei = [pw[:, k, c, bass.ds(i * PPT, PPT)].unsqueeze(2).to_broadcast([P, PPT, n]) for c in range(2)]
                        step(c1, c0, er, ALU.mult)
                        tt_(rtmp[:, 0, :, 0:n], s0, ei, ALU.mult)
                        tt_(s1, s0, er, ALU.mult)
                        tt_(rtmp[:, 1, :, 0:n], c0, ei, ALU.mult)
                        step(c1, c1, rtmp[:, 0, :, 0:n], ALU.subtract)
                        last = tt_(s1, s1, rtmp[:, 1, :, 0:n], ALU.add)
                    last.then_inc(tab_done, 1)
                    wait_alone(pool, bc_arrived, (tn + 1) * 16)
                    wait_alone(pool, y_done, tn * PPT + FREE2)
                    pool.drain()
                    fr, fi = [ff[:, c, bass.ds(i * PPT, PPT)].unsqueeze(2).to_broadcast([P, PPT, 32]) for c in range(2)]
                    cre, cim = [bc[:, 2 + c, :].rearrange("p (k n) -> p k n", k=PPT) for c in range(2)]
                    o_re, o_im = [cf[:, c, :].rearrange("p (k n) -> p k n", k=PPT) for c in range(2)]
                    s1 = rtmp[:, 0, :, 0:32]
                    tt_(o_re, cre, fr, ALU.mult)
                    tt_(s1, cim, fi, ALU.mult)
                    step(o_re, o_re, s1, ALU.subtract)
                    step(s1, cim, fr, ALU.mult)
                    tt_(o_im, cre, fi, ALU.mult)
                    step(o_im, o_im, s1, ALU.add)
                    ts_(o_im, o_im, -1.0).then_inc(cf_done, 1)

                    def head_rms(hn):
                        wait_alone(pool, ss_done, hn + 1)
                        ts_(rms[:, :], ss[:, :], 1.0 / P, LN_EPS, ALU.mult, ALU.add)
                        step(rms[:, :], rms[:, :], halfc[:, 0, 0:2], ALU.pow).then_inc(rms_done, 1)

                    def pair_sum(pn, pp):
                        wait_alone(pool, pq_done, pn + 1 + FREE)
                        pq = pq2[:, pp % 2]
                        tt_(pq[:, 0, :], pq[:, 0, :], pq[:, 3, :], ALU.add)
                        tt_(pq[:, 1, :], pq[:, 1, :], pq[:, 2, :], ALU.subtract).then_inc(r_done, 1)

                    pn, hn = li * PAIRS + i * PPT, li * HEADS + i * 2
                    pair_sum(pn, 0)
                    head_rms(hn)
                    for pp in (1, 2, 3):
                        pair_sum(pn + pp, pp)
                    head_rms(hn + 1)
                norm_rstd(li * 2 + 1)
            norm_rstd(2 * DEPTH)

        @block.tensor
        def _(pe):
            def products(turn, j, lhs, kt0, a, first, last, units=None):
                t, s = slot(turn, j)
                pe.wait_ge(lo_ready[s], t + 1 + FREE)
                for tt in range(TT):
                    if units is not None:
                        pe.wait_ge(t_lo, units + tt + 1 + FREE2)
                    o = acc[a][:, tt, :]
                    for k in range(CK):
                        hi = lhs[0][:, kt0 + k, tt * P:(tt + 1) * P]
                        lo = lhs[1][:, kt0 + k, tt * P:(tt + 1) * P]
                        nc.tensor.matmul(o, hi, whi[:, s, k], start=first and k == 0, stop=False)
                        nc.tensor.matmul(o, hi, wlo[:, s, k], start=False, stop=False)
                        i_ = nc.tensor.matmul(o, lo, whi[:, s, k], start=False, stop=last and k == CK - 1)
                    if last and tt == 0:
                        i_.then_inc(half_done, 1)
                i_.then_inc(chunk_used[s], 1)

            def t_units(u0, src, ready, count):
                for tt in range(TT):
                    pe.wait_ge(ready, count[tt])
                    pe.wait_ge(t_lo, u0 + tt - 1 + FREE2)
                    for q in range(4):
                        i_ = nc.tensor.transpose(S[tt][:, q * P:(q + 1) * P], src[:, tt, q * P:(q + 1) * P], ident)
                    i_.then_inc(t_bank, 1)

            def norm_units(q, n, u0):
                done = q * (2 * NSL) + 2 * n + FREE
                t_units(u0 + 2 * n, h[:, :, n * NS:(n + 1) * NS], norm_out, (done + 1, done + 2))

            def norm_and_products(q, u0, turn, a):
                norm_units(q, 0, u0)
                for j in range(CPS):
                    products(turn, j, aT, CK * j, a, j == 0, j == CPS - 1, u0 + 2 * (j // 2))
                    if j % 2 == 0 and j // 2 + 1 < NSL:
                        norm_units(q, j // 2 + 1, u0)

            def head_step(st, hn, hd):
                if st == "scores":
                    pe.wait_ge(q_copied, hn + 1)
                    for qt in range(2):
                        w = (qt + 1) * P
                        for c in range(2):
                            r = slice(c * QK, (c + 1) * QK)
                            nc.tensor.matmul(S[c][:, qt * P:qt * P + w], qs[r, 0, qt * P:(qt + 1) * P],
                                             qs[r, 1, 0:w], start=True, stop=True)
                            i_ = nc.tensor.matmul(S[c][:, 2 * qt * P:(2 * qt + 1) * P], identb[:, :], maskb[:, :], start=False,
                                                  stop=True, skip_group_check=True)
                    i_.then_inc(score_done, 1)
                elif st == "transpose":
                    pe.wait_ge(at_done, hn + 1)
                    for b in range(3):
                        i_ = nc.tensor.transpose(S[0][:, b * P:(b + 1) * P], ats[:, b * P:(b + 1) * P], ident)
                    i_.then_inc(atT_done, 1)
                elif st == "values":
                    pe.wait_ge(atT_copied, hn + 1)
                    nc.tensor.matmul(S[1][:, 0:P], atT[:, 0:P], v[:, 0, bass.ds(hd * P, P)], start=True, stop=True)
                    nc.tensor.matmul(S[1][:, P:2 * P], atT[:, P:2 * P], v[:, 0, bass.ds(hd * P, P)], start=True, stop=False)
                    nc.tensor.matmul(S[1][:, P:2 * P], atT[:, 2 * P:3 * P], v[:, 1, bass.ds(hd * P, P)], start=False,
                                     stop=True).then_inc(pv_done, 1)
                elif st == "out":
                    pe.wait_ge(o_done, hn + 1)
                    for qt in range(2):
                        i_ = nc.tensor.transpose(S[0][:, qt * P:(qt + 1) * P], osb[:, qt, :], ident)
                    i_.then_inc(oT_done, 1)

            def pair_step(st, pn, i, pp, tn):
                r = slice(32 * pp, 32 * (pp + 1))
                if st == 0:
                    if pp == 0:
                        pe.wait_ge(bc_arrived, (tn + 1) * 16)
                        pe.wait_ge(u_copied, tn + 1)
                    pe.wait_ge(pq_done, pn + FREE)
                    for c in range(2):
                        i_ = nc.tensor.matmul(S[2][:, c * SEQ:(c + 1) * SEQ], bc[r, c, :], gl[r, 0, :], start=True, stop=True)
                    i_.then_inc(bu_done, 1)
                else:
                    if pp == 0:
                        pe.wait_ge(cf_done, tn + 1 + FREE)
                    pe.wait_ge(xx_done, pn + 1 + FREE)
                    for c in range(2):
                        i_ = nc.tensor.matmul(S[3][r, 0:SEQ], cf[:, c, r], pq2[:, pp % 2, c, :], start=(c == 0), stop=(c == 1))
                    i_.then_inc(y_done, 1)

            for x_ in (*chunk_used, bu_done, y_done, y_done):
                pe.sem_inc(x_, FREE)
            pe.wait_ge(cst_arrived, 32)
            pe.wait_ge(mask_ready, 1)
            with pe.Fori(0, DEPTH) as li:
                turn = li * lay
                pair = li * layp
                u_in = li * U_LAYER

                def bank_free(pair, k):
                    pe.wait_ge(*taken(pair, k - 2))

                for r in range(8):
                    b = r % 2
                    bank_free(pair, r)
                    if r == 0:
                        norm_and_products(li * 2, u_in, turn, b)
                    for j in range(CPS):
                        if r > 0:
                            products(turn + 2 * r, j, aT, CK * j, b, j == 0, j == CPS - 1)
                        if j == 1 and (r == 1 or 3 <= r <= 6):
                            xu = li * X_UNITS + (0 if r == 1 else 2 * (r - 2))
                            pe.wait_ge(x_out, xu + FREE)
                            if r == 1:
                                pe.wait_ge(*taken(pair, 0))
                            else:
                                pe.wait_ge(rope_done, li * 4 + r - 2)
                            for tt in range(TT):
                                for q in range(4):
                                    i_ = nc.tensor.transpose(S[2 + tt][:, q * P:(q + 1) * P],
                                                             stg[:, (r - 1) % 2, tt, q * P:(q + 1) * P], ident)
                                i_.then_inc(x_bank, 1)
                        if r == 2 and j == 1:
                            pe.wait_ge(*taken(pair, 1))
                            pe.wait_ge(mt_arrived, (li + 1) * 16)
                            pe.wait_ge(x_out, li * X_UNITS + 2 + FREE)
                            for g in range(CT):
                                o = S[2 + g // 2][:, (g % 2) * SEQ:(g % 2 + 1) * SEQ]
                                cg = slice(g * P, (g + 1) * P)
                                nc.tensor.matmul(o[:, 0:P], stg[:, 1, 0, cg], mt[:, g, 0, :], start=True, stop=True)
                                nc.tensor.matmul(o[:, P:SEQ], stg[:, 1, 0, cg], mt[:, g, 1, :], start=True, stop=False)
                                i_ = nc.tensor.matmul(o[:, P:SEQ], stg[:, 1, 1, cg], mt[:, g, 2, :], start=False, stop=True)
                            i_.then_inc(p_mean, 1)
                        if r == 2 and j == 3:
                            pe.wait_ge(p_copy, li + 1)
                            pe.wait_ge(cp_arrived, (li + 1) * 32)
                            for g in range(CT):
                                i_ = nc.tensor.matmul(S[2 + g // 2][:, (g % 2) * SEQ:(g % 2 + 1) * SEQ], poolw[:, g, :],
                                                      pq[:, g, :], start=True, stop=True)
                            i_.then_inc(p_mix, 1)
                        if r == 3 and j == 0:
                            pe.wait_ge(p_lo, li + 1)
                with pe.Fori(0, CT // 2) as ii:
                    tg = turn + C_GATE // RING + ii * 12
                    for jj in range(6 * CPS):
                        i, j, k = ii * 2 + jj // TILE, jj % TILE, jj // CPS
                        tn = li * CT + i
                        if j % CPS == 0:
                            bank_free(pair + ii * 3, G_GATE + k)
                        products(tg, jj, aT, CK * (j % CPS), k % 2, j % CPS == 0, j % CPS == CPS - 1)
                        for hh in range(HPT):
                            if j - HEAD_SHIFT * hh in HEAD_PE:
                                head_step(HEAD_PE[j - HEAD_SHIFT * hh], li * HEADS + i * HPT + hh, i * HPT + hh)
                        if j in PAIR_Y:
                            pp = PAIR_Y.index(j)
                            pair_step(1, li * PAIRS + i * PPT + pp, i, pp, tn)
                        if j in PAIR_BU:
                            pp = PAIR_BU.index(j)
                            pair_step(0, li * PAIRS + i * PPT + pp, i, pp, tn)
                for n in range(NSL):
                    tp = turn + C_PROJ // RING + 2 * n
                    for j in range(CPS):
                        if j in (0, 4, 6):
                            q = 3 * n + (0, 4, 6).index(j)
                            bank_free(pair, G_PROJ + q)
                        if n == 0 and j == 0:
                            pe.wait_ge(o_lo, (li + 1) * HEADS)
                        if n == 0 and j == 6:
                            pe.wait_ge(glu_lo, li + 1)
                        products(tp, j, yT, CK * j, q % 2, j in (0, 4, 6), j in (3, 5, 7))
                        if n == 0 and j < 2:
                            if j == 0:
                                pe.wait_ge(glu_arrived, (li + 1) * 16)
                                pe.wait_ge(y2_done, (li + 1) * CT + FREE)
                            for ot in (2 * j, 2 * j + 1):
                                for k in range(CT):
                                    i_ = nc.tensor.matmul(S[2 + j][:, (ot % 2) * SEQ:(ot % 2 + 1) * SEQ],
                                                          gluw[:, k, ot * P:(ot + 1) * P], uT[:, k, :], start=(k == 0),
                                                          stop=(k == CT - 1))
                            i_.then_inc(glu_mm, 1)
                        if n > 0 and j == 1:
                            t_units(u_in + U_MERGE + 2 * (n - 1), merged, merge_done, [li * MERGES + 2 * n] * TT)
                for n in range(NSL):
                    tw = turn + C_WOUT // RING + 2 * n
                    bank_free(pair, G_WOUT + n)
                    for j in range(CPS):
                        need = u_in + U_MERGE + 2 * (j // 2) if n == 0 else None
                        products(tw, j, aT, CK * j, n % 2, j == 0, j == CPS - 1, need)
                        if n == 0 and j == 1:
                            t_units(u_in + U_MERGE + 6, merged, merge_done, [li * MERGES + 8] * TT)

                def hidden_group(g, first):
                    tm = turn + C_MLP // RING + g * 16
                    um = u_in + U_MLP + g * 8
                    for n in range(2 * NSL):
                        up = n < NSL
                        bank_free(pair + g * NSL, G_MLP + n)
                        if n == 0 and first:
                            norm_and_products(li * 2 + 1, u_in + U_LN1, tm, 0)
                        else:
                            for j in range(CPS):
                                need = um + 2 * (j // 2) if n == NSL else None
                                products(tm + 2 * n, j, aT if up else yT, CK * j, n % 2, j == 0, j == CPS - 1, need)
                                if 0 < n <= NSL and j == 1:
                                    t_units(um + 2 * (n - 1), stg[:, (n - 1) % 2], hid_done,
                                            [(li * FF_GROUPS + g) * NSL + n] * TT)

                hidden_group(0, True)
                with pe.Fori(1, FF_GROUPS) as g:
                    hidden_group(g, False)


def _constants():
    c = np.zeros((P, CC_N), np.float32)
    c[:, CC_IDENT:CC_IDENT + P] = np.eye(P, dtype=np.float32)
    c[:, CC_MASK:CC_MASK + P] = np.where(np.arange(P)[None, :] > np.arange(P)[:, None], MASKED, 0.0)
    s, t = np.arange(SEQ)[:, None], np.arange(SEQ)[None, :]
    for g, w in enumerate(POOL_WINDOWS):
        m = ((s <= t) & (s > t - w)) / np.minimum(t + 1, w) - (s == t)
        for b, (a0, b0) in enumerate(((0, 0), (0, P), (P, P))):
            o = CC_MT + (g * 3 + b) * P
            c[:, o:o + P] = m[a0:a0 + P, b0:b0 + P]
    f = np.float32(ROPE_THETA) ** (-np.arange(0, ROT, 2, dtype=np.float32) / np.float32(ROT))
    c[:, CC_FREQ:CC_MT] = f.astype(np.float32)
    return c


def _columns(a, lam):
    out = np.zeros((DEPTH, P, PC_N), np.float32)
    st = lambda z: z.reshape(DEPTH, PAIRS, P).transpose(0, 2, 1)
    out[:, :, PC_AR:PC_AR + PAIRS] = st(a["ssm_a_re"])
    out[:, :, PC_AI:PC_AI + PAIRS] = st(a["ssm_a_im"])
    out[:, :, PC_LDT:PC_LDT + PAIRS] = st(np.repeat(a["ssm_log_dt"][:, :, None], SSM_STATE, 2))
    for c, n in ((PC_D, "ssm_d"), (PC_GLUB, "glu_b"), (PC_PSC, "pool_scale")):
        out[:, :, c:c + CT] = a[n].reshape(DEPTH, CT, P).transpose(0, 2, 1)
    out[:, :, PC_SUBG] = a["subln_g"]
    out[:, :, PC_LAMC:PC_LAMC + 2] = lam[:, None, :]
    for k, n in enumerate(("lam_q1", "lam_q2", "lam_k1", "lam_k2")):
        out[:, :, PC_LAM + k * QK:PC_LAM + (k + 1) * QK] = a[n][:, None, :]
    return out


def _ssm_blocks(a):
    out = np.zeros((DEPTH, CT, P, 4, P), np.float32)
    for k, n in enumerate(("ssm_b_re", "ssm_b_im")):
        b = a[n].reshape(DEPTH, CT, PPT, 2, SSM_STATE, SSM_CH)
        for pp in range(PPT):
            for e in range(2):
                r = pp * 32 + e * SSM_CH
                out[:, :, r:r + SSM_CH, k, e * SSM_STATE:(e + 1) * SSM_STATE] = b[:, :, pp, e].transpose(0, 1, 3, 2)
    for k, n in enumerate(("ssm_c_re", "ssm_c_im")):
        c = a[n].reshape(DEPTH, CT, PPT, 2, SSM_CH, SSM_STATE)
        for pp in range(PPT):
            for e in range(2):
                r = pp * 32 + e * SSM_CH
                out[:, :, e * SSM_STATE:(e + 1) * SSM_STATE, 2 + k, r:r + SSM_CH] = c[:, :, pp, e].transpose(0, 1, 3, 2)
    return out


def kernel(**inputs):
    import concourse.bacc as bacc
    from concourse.bass_utils import run_bass_kernel_spmd

    a = {n: np.ascontiguousarray(z) for n, z in inputs.items()}
    init = [0.8 - 0.6 * math.exp(-0.3 * l) for l in range(DEPTH)]
    lam = np.array([[z, 1.0 - z] for z in init], np.float32)
    arrays = {
        "x": a["x"].reshape(SEQ, D_MODEL),
        "pos": np.ascontiguousarray(a["positions"].reshape(TT, P).T),
        "ln_top": np.concatenate([np.stack([a["ln_in_g"], a["ln_in_b"]])[None], np.stack([a["ln2_g"], a["ln2_b"]], 1)]),
        "w_in": a["w_in"], "b_gate": a["b_gate"],
        "colp": _columns(a, lam),
        "pool_w": a["pool_w"],
        "ssm_bc": _ssm_blocks(a),
        "glu_w": a["glu_w"], "proj_attn": a["proj_attn"], "proj_pool": a["proj_pool"], "proj_ssm": a["proj_ssm"],
        "w_out": a["w_out"],
        "ln1": np.stack([a["ln1_g"], a["ln1_b"]], 1),
        "w_up": a["w_up"], "w_down": a["w_down"],
        "consts": _constants(),
    }
    nc = bacc.Bacc("TRN2", target_bir_lowering=False, num_devices=1, dynamic_dma_scratch_size=1024)
    args = [nc.dram_tensor(f"{n}_dram", z.shape, mybir.dt.from_np(z.dtype), kind="ExternalInput").ap()
            for n, z in arrays.items()]
    gates = nc.dram_tensor("gates_dram", (TT, P, 3 * D_MODEL), mybir.dt.float32, kind="Internal").ap()
    out = nc.dram_tensor("out_dram", (SEQ, D_MODEL), mybir.dt.float32, kind="ExternalOutput").ap()
    build_trunk(nc, *args, gates, out)
    r = run_bass_kernel_spmd(nc, [{f"{n}_dram": z for n, z in arrays.items()}], core_ids=[0])
    return r.results[0]["out_dram"].reshape(1, SEQ, D_MODEL)
```
